# Optimizing a Trainium2 kernel written in Bass

```python
import jax, jax.numpy as jnp
from jax import lax
import numpy as np

D_MODEL = 1024
BATCH = 1
SEQ = 2048
DEPTH = 1

GDN_HEAD_DIM = 128
GDN_WIDTH = D_MODEL // 2
GDN_HEADS = GDN_WIDTH // GDN_HEAD_DIM
GDN_CONV = 4
CHUNK = 64
SC_WIDTH = D_MODEL - GDN_WIDTH
SC_GROUPS = 8
SC_CONV = 3
MIX_WIDTH = GDN_WIDTH + SC_WIDTH
IN_COLS = 4 * GDN_WIDTH + 2 * GDN_HEADS + 3 * SC_WIDTH
N_MEM = 256
XATTN_HEADS = 4
XATTN_HEAD_DIM = D_MODEL // XATTN_HEADS
D_FF = ((8 * D_MODEL + 3 * 256 - 1) // (3 * 256)) * 256
EPS = 1e-6

kernel_name = "hybrid_gdn_shortconv_memxattn_block"

def rms_norm(x, g):
    xf = x.astype(jnp.float32)
    y = xf * lax.rsqrt(jnp.mean(xf * xf, axis=-1, keepdims=True) + EPS)
    return (y * g.astype(jnp.float32)).astype(x.dtype)

def l2norm(x):
    return x * lax.rsqrt(jnp.sum(x * x, axis=-1, keepdims=True) + EPS)

def causal_depthwise_conv(x, w):
    K, C = w.shape
    return lax.conv_general_dilated(
        x, w[:, None, :].astype(x.dtype), window_strides=(1,), padding=[(K - 1, 0)],
        dimension_numbers=('NWC', 'WIO', 'NWC'), feature_group_count=C)

def gated_delta_rule_chunked(q, k, v, g, beta):
    B, S, H, dk = q.shape
    dv = v.shape[-1]
    N = S // CHUNK

    def to_chunks(t):
        t = t.reshape((B, N, CHUNK, H) + t.shape[3:])
        return jnp.moveaxis(t, 3, 1)

    q, k, v, g, beta = (to_chunks(t) for t in (q, k, v, g, beta))
    q = q * (dk ** -0.5)
    gc = jnp.cumsum(g, axis=-1)
    idx = jnp.arange(CHUNK)
    causal = idx[:, None] >= idx[None, :]
    strict = idx[:, None] > idx[None, :]
    diff = gc[..., :, None] - gc[..., None, :]
    decay = jnp.exp(jnp.where(causal, diff, -jnp.inf))
    k_beta = k * beta[..., None]
    A = jnp.where(strict, jnp.einsum('bhnid,bhnjd->bhnij', k_beta, k) * decay, 0.0)
    eye = jnp.eye(CHUNK, dtype=q.dtype)
    T = lax.linalg.triangular_solve(eye + A, jnp.broadcast_to(eye, A.shape),
                                    left_side=True, lower=True)
    u = jnp.einsum('bhnij,bhnjd->bhnid', T, v * beta[..., None])
    w = jnp.einsum('bhnij,bhnjd->bhnid', T, k_beta * jnp.exp(gc)[..., None])
    attn_qk = jnp.einsum('bhnid,bhnjd->bhnij', q, k) * decay
    q_dec = q * jnp.exp(gc)[..., None]
    g_last = gc[..., -1]
    k_dec = k * jnp.exp(g_last[..., None] - gc)[..., None]

    def step(state, inp):
        u_n, w_n, a_n, qd_n, kd_n, gl_n = inp
        v_new = u_n - jnp.einsum('bhcd,bhde->bhce', w_n, state)
        o = (jnp.einsum('bhcd,bhde->bhce', qd_n, state)
             + jnp.einsum('bhij,bhje->bhie', a_n, v_new))
        state = state * jnp.exp(gl_n)[..., None, None] + jnp.einsum('bhcd,bhce->bhde', kd_n, v_new)
        return state, o

    xs = tuple(jnp.moveaxis(t, 2, 0) for t in (u, w, attn_qk, q_dec, k_dec, g_last))
    state0 = jnp.zeros((B, H, dk, dv), jnp.float32)
    _, o = lax.scan(step, state0, xs)
    return jnp.transpose(o, (1, 0, 3, 2, 4)).reshape(B, S, H, dv)

def hybrid_mixer(xn, w_in, conv_qkv_w, a_log, dt_bias, gdn_norm_g, conv_sc_w, sc_norm_g, w_out):
    B, S, _ = xn.shape
    f32 = jnp.float32
    proj = xn @ w_in
    cuts = [3 * GDN_WIDTH, 4 * GDN_WIDTH, 4 * GDN_WIDTH + GDN_HEADS,
            4 * GDN_WIDTH + 2 * GDN_HEADS, 4 * GDN_WIDTH + 2 * GDN_HEADS + SC_WIDTH,
            4 * GDN_WIDTH + 2 * GDN_HEADS + 2 * SC_WIDTH]
    qkv, z, a, b, sc_b, sc_c, sc_h = jnp.split(proj, cuts, axis=-1)

    qkv = jax.nn.silu(causal_depthwise_conv(qkv, conv_qkv_w))
    q, k, v = jnp.split(qkv, 3, axis=-1)
    heads = lambda t: t.reshape(B, S, GDN_HEADS, GDN_HEAD_DIM).astype(f32)
    q, k, v = l2norm(heads(q)), l2norm(heads(k)), heads(v)
    g = -jnp.exp(a_log.astype(f32)) * jax.nn.softplus(a.astype(f32) + dt_bias.astype(f32))
    beta = jax.nn.sigmoid(b.astype(f32))
    o = gated_delta_rule_chunked(q, k, v, g, beta)
    o = rms_norm(o, gdn_norm_g) * jax.nn.silu(heads(z))
    o_gdn = o.reshape(B, S, GDN_WIDTH).astype(xn.dtype)

    y = sc_b * causal_depthwise_conv(sc_c * sc_h, conv_sc_w)
    y = rms_norm(y.reshape(B, S, SC_GROUPS, SC_WIDTH // SC_GROUPS),
                 sc_norm_g.reshape(SC_GROUPS, SC_WIDTH // SC_GROUPS)).reshape(B, S, SC_WIDTH)

    return jnp.concatenate([o_gdn, y.astype(xn.dtype)], axis=-1) @ w_out

def memory_cross_attention(hn, memn, w_xq, w_xk, w_xv, w_xo):
    B, S, _ = hn.shape
    M = memn.shape[1]
    q = (hn @ w_xq).reshape(B, S, XATTN_HEADS, XATTN_HEAD_DIM)
    k = (memn @ w_xk).reshape(B, M, XATTN_HEADS, XATTN_HEAD_DIM)
    v = (memn @ w_xv).reshape(B, M, XATTN_HEADS, XATTN_HEAD_DIM)
    s = jnp.einsum('bshd,bmhd->bhsm', q, k).astype(jnp.float32) * (XATTN_HEAD_DIM ** -0.5)
    p = jax.nn.softmax(s, axis=-1).astype(v.dtype)
    o = jnp.einsum('bhsm,bmhd->bshd', p, v).reshape(B, S, XATTN_HEADS * XATTN_HEAD_DIM)
    return o @ w_xo

def swiglu(hn, w_gate, w_up, w_down):
    return (jax.nn.silu(hn @ w_gate) * (hn @ w_up)) @ w_down

def setup_inputs(seed: int = 0) -> dict:
    key = jax.random.key(seed)
    ks = jax.random.split(key, 24)
    f32 = jnp.float32
    L = DEPTH

    def dense(k, fan_in, shape):
        return jax.random.normal(k, shape, f32) * (fan_in ** -0.5)

    def gain(k, n):
        return 1.0 + 0.02 * jax.random.normal(k, (L, n), f32)

    dt = jnp.exp(jax.random.uniform(ks[5], (L, GDN_HEADS), f32, np.log(1e-3), np.log(1e-1)))
    return {
        "x": jax.random.normal(ks[0], (BATCH, SEQ, D_MODEL), f32),
        "mem": jax.random.normal(ks[1], (BATCH, N_MEM, D_MODEL), f32),
        "norm_mix_g": gain(ks[2], D_MODEL),
        "w_in": dense(ks[3], D_MODEL, (L, D_MODEL, IN_COLS)),
        "conv_qkv_w": dense(ks[4], GDN_CONV, (L, GDN_CONV, 3 * GDN_WIDTH)),
        "a_log": jnp.log(jax.random.uniform(ks[6], (L, GDN_HEADS), f32, 1.0, 16.0)),
        "dt_bias": dt + jnp.log(-jnp.expm1(-dt)),
        "gdn_norm_g": gain(ks[7], GDN_HEAD_DIM),
        "conv_sc_w": dense(ks[8], SC_CONV, (L, SC_CONV, SC_WIDTH)),
        "sc_norm_g": gain(ks[9], SC_WIDTH),
        "w_out": dense(ks[10], MIX_WIDTH, (L, MIX_WIDTH, D_MODEL)),
        "norm_x_g": gain(ks[11], D_MODEL),
        "norm_mem_g": gain(ks[12], D_MODEL),
        "w_xq": dense(ks[13], D_MODEL, (L, D_MODEL, D_MODEL)),
        "w_xk": dense(ks[14], D_MODEL, (L, D_MODEL, D_MODEL)),
        "w_xv": dense(ks[15], D_MODEL, (L, D_MODEL, D_MODEL)),
        "w_xo": dense(ks[16], D_MODEL, (L, D_MODEL, D_MODEL)),
        "norm_ffn_g": gain(ks[17], D_MODEL),
        "w_gate": dense(ks[18], D_MODEL, (L, D_MODEL, D_FF)),
        "w_up": dense(ks[19], D_MODEL, (L, D_MODEL, D_FF)),
        "w_down": dense(ks[20], D_FF, (L, D_FF, D_MODEL)),
        "norm_final_g": 1.0 + 0.02 * jax.random.normal(ks[21], (D_MODEL,), f32),
    }

def reference(x, mem, norm_mix_g, w_in, conv_qkv_w, a_log, dt_bias, gdn_norm_g, conv_sc_w,
              sc_norm_g, w_out, norm_x_g, norm_mem_g, w_xq, w_xk, w_xv, w_xo, norm_ffn_g,
              w_gate, w_up, w_down, norm_final_g):
    h = x
    for l in range(DEPTH):
        h = h + hybrid_mixer(rms_norm(h, norm_mix_g[l]), w_in[l], conv_qkv_w[l], a_log[l],
                             dt_bias[l], gdn_norm_g[l], conv_sc_w[l], sc_norm_g[l], w_out[l])
        h = h + memory_cross_attention(rms_norm(h, norm_x_g[l]), rms_norm(mem, norm_mem_g[l]),
                                       w_xq[l], w_xk[l], w_xv[l], w_xo[l])
        h = h + swiglu(rms_norm(h, norm_ffn_g[l]), w_gate[l], w_up[l], w_down[l])
    return rms_norm(h, norm_final_g)


_drawn_inputs = setup_inputs


def setup_inputs(seed=0):
    import zlib

    import numpy as np

    out = dict(_drawn_inputs(seed))
    spreads = {}
    factors = {'gdn_norm_g': 7.845,
     'sc_norm_g': 4.825,
     'norm_x_g': 8.0,
     'norm_mem_g': 8.0,
     'norm_ffn_g': 4.748,
     'norm_final_g': 2.747}
    for name, (base, spread) in spreads.items():
        noise = np.random.default_rng([zlib.crc32(name.encode()), seed]).standard_normal(out[name].shape)
        drawn = base * np.exp(spread * noise) if base else spread * noise
        out[name] = __import__('jax').numpy.asarray(drawn.astype(out[name].dtype))
    for name, factor in factors.items():
        out[name] = (out[name] * factor).astype(out[name].dtype)
    return out
```

```python
import concourse.bass as bass
from concourse import mybir
from contextlib import ExitStack

f32 = mybir.dt.float32
f32r = mybir.dt.float32r
ACT = mybir.ActivationFunctionType
ALU = mybir.AluOpType
AX = mybir.AxisListType

P = 128
SEQ = 2048
D = 1024
KT = D // P
HALF = 1024
NHALF = SEQ // HALF
TT = HALF // P
CH = 512
NCH = HALF // CH
NH = 4
HD = 128
N_MEM = 256
XH = 4
XD = D // XH
FF = 2816
NPAIR = FF // (2 * P)
EPS = 1e-6
LEVELS = 7

MEM_UNITS = 2 * KT
QKVZ_UNITS = 4 * NH
MIX_UNITS = 3 * 4
OUT_UNITS = KT
ATT_UNITS = 4 * XH
FFN_UNITS = 6 * NPAIR
HALF_UNITS = QKVZ_UNITS + MIX_UNITS + OUT_UNITS + ATT_UNITS + FFN_UNITS
RING = 4
CONSTS = 34
GD = {n: i + 1 for i, n in enumerate(
    "copy a neg min bmin w1 wm eq mx rc l1 l2 l3 sp g b1 b2 gc gl fd nb nn".split())}
GATE_DVE = len(GD)
GATE_ACT = 6
CONV_OUT = [1 + g // 4 for g in range(6)]
CONV_OUT_PER = [2, 2, 1, 1]
SC_NORM_STEP = (33, 39)

ROW_PASSES = KT // 2 + XH + NPAIR
STEPS = 20
SLICES = 3 * NCH * KT
FIRST_SLICES = 6


def slices_before(step):
    last = 2 * STEPS - 2
    return min(SLICES, FIRST_SLICES + (SLICES - FIRST_SLICES) * step // last)


def groups_after(step):
    a, b = slices_before(step), slices_before(step + 1)
    return [g for g in range(3 * NCH) if a < (g + 1) * KT <= b]


def block_kernel(nc, x, mem, w_units, w_ab, conv_w, sc_w, a_log, dt_bias, gdn_g, sc_g,
                 g_mix, g_mem, g_x, g_ffn, g_fin, out):
    ctx = ExitStack()
    with ctx:
        cursor = [16512]

        def sb(name, shape, dt=f32, at=None):
            size = 4
            for s in shape[1:]:
                size *= s
            size = (size + 31) // 32 * 32
            if at is None:
                at = cursor[0]
                cursor[0] += size
            else:
                at, at_list = at[0], at
                at_list[0] += size
            assert at + size <= 229344, (name, at + size)
            return nc.alloc_sbuf_tensor_at(name, shape, dt, offset=at)

        def sem(name):
            return ctx.enter_context(nc.semaphore(name))

        ident = sb("ident", [P, P])
        ones = sb("ones", [P, P])
        group_ones = sb("group_ones", [P, P])
        upto = sb("upto", [P, P])
        level_mask = sb("level_mask", [P, LEVELS, P])
        gain = sb("gain", [P, D])
        wab_hi = sb("wab_hi", [P, KT * 8 + P], f32r)
        wab_lo = sb("wab_lo", [P, KT * 8 + P], f32r)
        cw = sb("cw", [P, NH, 3, 4])
        scw = sb("scw", [P, 4, 3])
        scg = sb("scg", [P, 4, 1])
        gdng = sb("gdng", [P, 1])
        nega = sb("nega", [P, NH])
        dtb = sb("dtb", [P, NH])
        halo = sb("halo", [P, NH, 3, 3])
        sc_halo = sb("sc_halo", [P, 4, 2])
        state = sb("state", [P, NH, HD])
        kmem = sb("kmem", [P, KT, N_MEM])
        gate_ab = sb("gate_ab", [P, TT, 8])
        G = {k: sb("gate_" + k, [P, TT, NH]) for k in
             ("t0", "t1", "t2", "t3", "t4", "g", "gc", "beta", "nbeg", "fdec", "elast", "egc")}
        stat = {k: sb("stat_" + k, [P, 2]) for k in ("ss", "t", "l", "y", "u", "v", "r")}
        act_hi = sb("act_hi", [P, KT, HALF], f32r)
        act_lo = sb("act_lo", [P, KT, HALF], f32r)
        w_hi = [sb(f"w_hi{i}", [P, D], f32r) for i in range(RING)]
        w_lo = [sb(f"w_lo{i}", [P, D], f32r) for i in range(RING)]
        raw = [sb(f"raw{i}", [P, D]) for i in range(3)]
        overlay = cursor[0]
        row_hi = sb("row_hi", [P, 2, HALF], f32r)
        row_lo = sb("row_lo", [P, 2, HALF], f32r)
        w_hi += [sb(f"w_hi{i}", [P, D], f32r) for i in (4, 5)]
        w_lo += [sb(f"w_lo{i}", [P, D], f32r) for i in (4, 5)]
        h = sb("h", [P, TT, D])
        temps = cursor[0]
        xn = sb("xn", [P, 2, D])
        z = [overlay + 32768]
        xin = sb("xin", [P, 2, D], at=z)
        conv_in = [sb(f"conv_in{i}", [P, 3 + HALF], at=z) for i in range(2)]
        conv_acc = sb("conv_acc", [P, 2, CH], at=z)
        stage = sb("stage", [P, 2, CH], at=z)
        ab_t = sb("ab_t", [P, HALF], at=[overlay])
        vmem = sb("vmem", [P, 2, D], at=[overlay])
        z = [overlay]
        sc_u = sb("sc_u", [P, 2 + HALF], at=z)
        sc_acc = sb("sc_acc", [P, CH], at=z)
        sc_y = sb("sc_y", [P, 2, CH], at=z)
        sc_sq = sb("sc_sq", [P, CH], at=z)
        qk = sb("qk", [P, 2, 2, NH, P], at=z)
        vv = sb("vv", [P, 2, NH, P], at=z)
        zz = sb("zz", [P, 2, NH, P], at=z)
        rn = sb("rn", [P, 2, NH, P], at=z)
        kqn = sb("kqn", [P, NH, 2, P], at=z)
        ge = sb("ge", [P, NH, P], at=z)
        diff = sb("diff", [P, NH, P], at=z)
        dec = sb("dec", [P, 2, NH, P], at=z)
        am = sb("am", [P, 2, NH, P], at=z)
        kbg = sb("kbg", [P, NH, P], at=z)
        kdec = sb("kdec", [P, NH, P], at=z)
        vb = sb("vb", [P, NH, P], at=z)
        Xm = sb("Xm", [P, NH, P], at=z)
        Tm = sb("Tm", [P, NH, P], at=z)
        Ym = sb("Ym", [P, NH, P], at=z)
        wt = sb("wt", [P, NH, P], at=z)
        vnew = sb("vnew", [P, NH, P], at=z)
        osq = sb("osq", [P, NH, P], at=z)
        on = osq
        oo = sb("oo", [P, NH, P], at=z)
        ost = {k: sb("ost_" + k, [P, NH], at=z) for k in ("ss", "t", "l", "y", "u", "v", "w", "r")}
        mixraw = xn
        z = [overlay + 16384]
        qT = sb("qT", [P, 2, HALF], at=z)
        pp = sb("pp", [P, 4, N_MEM], at=z)
        pT = sb("pT", [P, 2, CH], at=z)
        z = [cursor[0]]
        vh = sb("vh", [P, 2, XD], at=z)
        smx = sb("smx", [P, 3, 4], at=z)
        rsum = sb("rsum", [P, 4], at=z)
        z = [temps]
        sg = sb("sg", [P, 2, CH], at=z)
        aa = sb("aa", [P, 2, CH], at=z)
        PS = ctx.enter_context(nc.psum_tensor("PS", [P, 8, 512], f32))

        qkvz_d = nc.dram_tensor("qkvz_d", [4, NH, P, SEQ], f32, kind="Internal").ap()
        vmem_d = nc.dram_tensor("vmem_d", [P, 2, D], f32, kind="Internal").ap()
        mix_d = nc.dram_tensor("mix_d", [KT, P, SEQ], f32, kind="Internal").ap()

        S = {}

        def sems(names):
            for n in names.split():
                S[n] = sem(n)

        sems("const_in const_made nega_ready wab_raw wab_hi_ready wab_lo_ready gain_in")
        sems("raw_ready0 raw_ready1 raw_ready2 w_hi_ready w_lo_ready")
        sems("x_in0 x_in1 ss_ready ln_ready y_ready nstat xn_ready tr_full0 tr_full1 "
             "tr_hi tr_lo0 tr_lo1 out_stored0 out_stored1")
        sems("km_full0 km_full1 km_out0 km_out1 vm_full vm_out vm_stored")
        sems("ab_full0 ab_full1 ab_out abt_full gate_step_dve gate_step_act gate_gc_full")
        for b in range(4):
            sems(f"qkvz_full{b} qkvz_out{b}")
        sems("halo_in conv_step conv_ready halo_out stage_ready st_stored0 st_stored1")
        sems("ld0 ld1 sq_ready rln_ready rn_ready gu_ready diff_ready egb_ready relu_ready "
             "dec_ready decm_ready am_ready t1_ready kqn_ready qdec_ready kbg_ready kdec_ready "
             "vb_ready a_ready attn_ready x_ready t_ready ym_ready wt_ready vnew_ready s_ready "
             "osq_ready ossum_ready ost_ready oln_ready oy_ready ostep on_ready oo_ready o_stored")
        for b in range(4, 8):
            sems(f"gdn_full{b}")
        sems("sc_full0 sc_full1 sc_full2 scn_full c_out u_ready sc_halo_in sc_halo_out sc_step "
             "scy_ready scsq_ready scln_ready scr_ready scyn_ready y_stored state_zero")
        sems("row_full0 row_full1 row_out0 row_out1 h_in mix_in0 mix_in1 mix_hi_ready mix_lo_ready")
        sems("q_full q_out s_full mx_ready p_exp rs_ready p_ready pt_full pt_out vh_ready "
             "pv_full ot_hi ot_lo mx_step")
        sems("gu_full0 gu_full1 sg_ready ga_ready0 ga_ready1 ah_ready al_ready0 al_ready1")

        def bank(b, n=1):
            return PS[:, b:b + n, :] if n > 1 else PS[:, b, :]

        def flat(ap):
            return ap.rearrange("p a b -> p (a b)")

        def over_tokens(ap):
            return ap.unsqueeze(2).broadcast_to([P, NH, P])

        def over_heads(ap):
            return ap.unsqueeze(1).broadcast_to([P, NH, P])

        def r4(ap):
            return ap.rearrange("p (h t) -> p h t", h=NH)

        U_QKVZ = 0
        U_MIX = U_QKVZ + QKVZ_UNITS
        U_OUT = U_MIX + MIX_UNITS
        U_ATT = U_OUT + OUT_UNITS
        U_FFN = U_ATT + ATT_UNITS

        def unit(half, k):
            return MEM_UNITS + half * HALF_UNITS + k

        L_QKVZ = 0
        L_MIX = L_QKVZ + QKVZ_UNITS // 2
        L_OUT = L_MIX + MIX_UNITS // 3
        L_ATT = L_OUT + OUT_UNITS // 2
        L_FFN = L_ATT + ATT_UNITS // 2
        HALF_LOADS = L_FFN + FFN_UNITS // 2

        def nth_load(half, before):
            return MEM_UNITS // 2 + half * HALF_LOADS + before + 1

        R_OUT, R_ATT, R_FFN = 0, KT // 2, KT // 2 + XH

        def norm_no(half, which, t):
            return 2 + (half * 4 + which) * TT + t

        def transposed(half, which):
            return 1 + (half * 3 + which) * (TT // 2)

        def gdn_pool(pool, n, c, j, step):
            if step == 1:
                pool.wait_ge(S["dec_ready"], n + 1)
                pool.tensor_tensor(dec[:, 0, :, :], dec[:, 0, :, :],
                                   over_tokens(G["beta"][:, bass.ds(j * 2 + c, 1), :]
                                               .rearrange("p n h -> p (n h)")), ALU.mult)\
                    .then_inc(S["decm_ready"], 1)
                pool.tensor_tensor(dec[:, 1, :, :], dec[:, 1, :, :], over_heads(upto[:, :]),
                                   ALU.mult).then_inc(S["decm_ready"], 1)
            if step == 2:
                for l in range(LEVELS):
                    if l == 0:
                        pool.wait_ge(S["a_ready"], n + 1)
                    if l >= 2:
                        pool.wait_ge(S["gdn_full4"], n * 10 + 2 + l - 1)
                        if l == 2:
                            pool.wait_ge(S["t1_ready"], n + 1)
                    else:
                        pool.wait_ge(S["gdn_full4"], n * 10)
                    pool.tensor_tensor(am[:, l % 2, :, :], dec[:, 0, :, :],
                                       over_heads(level_mask[:, l, :]), ALU.mult)\
                        .then_inc(S["am_ready"], 1)
                    if l == 0:
                        pool.wait_ge(S["am_ready"], n * LEVELS + 1)
                        pool.tensor_tensor(Tm[:, :, :], over_heads(ident[:, :]), am[:, 0, :, :],
                                           ALU.subtract).then_inc(S["t1_ready"], 1)

        def ffn_pool(pool, half, j, split_lo, last):
            n_u = unit(half, U_FFN + j * 6)
            R = half * NPAIR + j
            for f in range(2):
                split_lo((n_u + 2 + 2 * f, 2 + 2 * f, 0))
                split_lo((n_u + 3 + 2 * f, 3 + 2 * f, 1))
                for c in range(2):
                    pool.wait_ge(S["ah_ready"], R * 4 + f * 2 + c + 1)
                    pool.tensor_tensor(row_lo[:, f, c * CH:(c + 1) * CH], aa[:, c, :],
                                       row_hi[:, f, c * CH:(c + 1) * CH].bitcast(f32),
                                       ALU.subtract).then_inc(S[f"al_ready{c}"], 1)
            if not last:
                split_lo((n_u + 6, 0, 0))
                split_lo((n_u + 7, 1, 1))

        def gates_act(act, half):
            dve, own = S["gate_step_dve"], S["gate_step_act"]
            k = half * GATE_ACT
            d = half * GATE_DVE
            act.wait_ge(dve, d + GD["min"])
            act.activation(G["t1"][:, :, :], G["t1"][:, :, :], ACT.Exp).then_inc(own, 1)
            act.wait_ge(dve, d + GD["bmin"])
            act.activation(G["beta"][:, :, :], G["beta"][:, :, :], ACT.Exp).then_inc(own, 1)
            act.wait_ge(dve, d + GD["w1"])
            act.activation(G["t3"][:, :, :], G["t2"][:, :, :], ACT.Ln).then_inc(own, 1)

        def gates_act_late(act, half):
            dve, own = S["gate_step_dve"], S["gate_step_act"]
            d = half * GATE_DVE
            act.wait_ge(dve, d + GD["fd"])
            act.activation(G["egc"][:, :, :], G["gc"][:, :, :], ACT.Exp).then_inc(own, 1)
            act.activation(G["elast"][:, :, :], G["t0"][:, :, :], ACT.Exp).then_inc(own, 1)
            act.activation(G["fdec"][:, :, :], G["t1"][:, :, :], ACT.Exp).then_inc(own, 1)

        def silu_store(act, half, j, R, g):
            u, c = g // 2, g % 2
            act.wait_ge(S["conv_ready"], R * 6 + g + 1)
            act.wait_ge(S[f"st_stored{c}"], (R * 4 + g // 2) * 16)
            act.activation(stage[:, c, :], conv_acc[:, c, :], ACT.Silu)\
                .then_inc(S["stage_ready"], 1)
            act.wait_ge(S["stage_ready"], R * 8 + g + 1)
            store_stage(act, half, j, u, c)

        def store_stage(act, half, j, u, c):
            act.dma_start(qkvz_d[u, bass.ds(j, 1), :, bass.ds(half * HALF + c * CH, CH)]
                          .rearrange("n p c -> p (n c)"), stage[:, c, :])\
                .then_inc(S[f"st_stored{c}"], 16)

        def silu_z(act, half, j, R, g):
            c, b = g % 2, g % 4
            act.wait_ge(S[f"qkvz_full{b}"], R * 2 + g // 4 + 1)
            act.wait_ge(S[f"st_stored{c}"], (R * 4 + 3) * 16)
            act.activation(stage[:, c, :], bank(b), ACT.Silu).then_inc(S["stage_ready"], 1)
            act.wait_ge(S["stage_ready"], R * 8 + g + 1)
            store_stage(act, half, j, 3, c)

        def load_chunk(act, half, n, local, c):
            act.wait_ge(S["oo_ready"], n - c)
            cols = bass.ds(half * HALF + local * P, P)
            for i in range(2):
                act.dma_start(qk[:, c, i, :, :], qkvz_d[i, :, :, cols].rearrange("h p t -> p h t"))\
                    .then_inc(S[f"ld{c}"], 16)
            act.dma_start(vv[:, c, :, :], qkvz_d[2, :, :, cols].rearrange("h p t -> p h t"))\
                .then_inc(S[f"ld{c}"], 16)
            act.dma_start(zz[:, c, :, :], qkvz_d[3, :, :, cols].rearrange("h p t -> p h t"))\
                .then_inc(S[f"ld{c}"], 16)

        def load_mix(act, half, kk):
            act.dma_start(mixraw[:, kk % 2, :],
                          mix_d[(kk + KT // 2) % KT, :, bass.ds(half * HALF, HALF)])\
                .then_inc(S[f"mix_in{kk % 2}"], 16)

        def loads(n, c):
            return (n - c) * 32 + 64

        def gdn_act_first(act, n, c):
            act.wait_ge(S[f"ld{c}"], loads(n, c))
            act.wait_ge(S["kqn_ready"], n * 2)
            act.activation(rn[:, :, :, :].rearrange("p a h t -> p (a h t)"),
                           qk[:, c, :, :, :].rearrange("p a h t -> p (a h t)"), ACT.Square)\
                .then_inc(S["sq_ready"], 1)

        def gdn_act(act, half, n, c, j, step):
            hflat = lambda t: t.rearrange("p h t -> p (h t)")
            if step == 0:
                act.wait_ge(S["gdn_full5"], n * 9 + 1)
                act.wait_ge(S["sq_ready"], n + 1)
                act.activation(rn[:, :, :, :].rearrange("p a h t -> p (a h t)"), flat(bank(4, 2)),
                               ACT.Ln, bias=EPS).then_inc(S["rln_ready"], 1)
                act.wait_ge(S["rln_ready"], n + 1)
                act.activation(rn[:, :, :, :].rearrange("p a h t -> p (a h t)"),
                               rn[:, :, :, :].rearrange("p a h t -> p (a h t)"), ACT.Exp,
                               scale=-0.5).then_inc(S["rn_ready"], 1)
                act.wait_ge(S["diff_ready"], n + 1)
                act.activation(hflat(ge[:, :, :]), bank(6), ACT.Exp).then_inc(S["egb_ready"], 1)
                act.wait_ge(S["gdn_full5"], n * 9)
                act.wait_ge(S["am_ready"], n * LEVELS)
                act.activation(hflat(dec[:, 0, :, :]), hflat(diff[:, :, :]), ACT.Relu)\
                    .then_inc(S["relu_ready"], 1)
                act.activation(hflat(dec[:, 1, :, :]), hflat(diff[:, :, :]), ACT.Relu, scale=-1.0)\
                    .then_inc(S["relu_ready"], 1)
                act.wait_ge(S["relu_ready"], n * 2 + 2)
                act.activation(dec[:, :, :, :].rearrange("p a h t -> p (a h t)"),
                               dec[:, :, :, :].rearrange("p a h t -> p (a h t)"), ACT.Exp,
                               scale=-1.0).then_inc(S["dec_ready"], 1)
            if 4 <= step < 16 and step % 2 == 0:
                l = (step - 2) // 2
                act.wait_ge(S["gdn_full4"], n * 10 + 2 + l + 1)
                if l >= 2:
                    act.wait_ge(S["gdn_full6"], n * 8 + 2 + l - 1)
                else:
                    act.wait_ge(S["gdn_full5"], n * 9)
                act.activation(hflat(Ym[:, :, :]), bank(4), ACT.Copy).then_inc(S["ym_ready"], 1)
            if step == 16:
                act.wait_ge(S["gdn_full7"], n * 3 + 2)
                act.wait_ge(S["gdn_full4"], n * 10 + 9)
                act.activation(hflat(wt[:, :, :]), bank(7), ACT.Copy).then_inc(S["wt_ready"], 1)
            if step == 17:
                act.wait_ge(S["gdn_full4"], n * 10 + 10)
                act.wait_ge(S["gdn_full6"], n * 8)
                act.activation(hflat(vnew[:, :, :]), bank(4), ACT.Copy)\
                    .then_inc(S["vnew_ready"], 1)
            if step == 18:
                act.wait_ge(S["gdn_full5"], n * 9 + 9)
                act.wait_ge(S["gdn_full7"], n * 3)
                act.activation(hflat(osq[:, :, :]), bank(5), ACT.Square)\
                    .then_inc(S["osq_ready"], 1)
                if c == 0:
                    gdn_act_first(act, n + 1, 1)
                act.wait_ge(S["ost_ready"], n + 1)
                act.activation(ost["l"][:, :], ost["t"][:, :], ACT.Ln).then_inc(S["oln_ready"], 1)
                act.wait_ge(S["oln_ready"], n + 1)
                act.activation(ost["y"][:, :], ost["l"][:, :], ACT.Exp, scale=-0.5)\
                    .then_inc(S["oy_ready"], 1)
            if step == 19:
                act.wait_ge(S["oo_ready"], n + 1)
                act.dma_start(mix_d[0:NH, :, bass.ds(half * HALF + (j * 2 + c) * P, P)]
                              .rearrange("h p t -> p h t"), oo[:, :, :])\
                    .then_inc(S["o_stored"], 16)

        def sc_act(act, half, j, g):
            R = half * 4 + j
            if g < 2:
                act.wait_ge(S[f"sc_full{g % 3}"], R * 2 + g // 3 + 1)
                act.wait_ge(S["sc_halo_out"], R)
                act.activation(sc_u[:, 2 + g * CH:2 + (g + 1) * CH], bank(g % 3), ACT.Copy)\
                    .then_inc(S["c_out"], 1)
            if g >= 4:
                c = g - 4
                act.wait_ge(S["scy_ready"], R * 2 + c + 1)
                act.wait_ge(S["scyn_ready"], R * 2 + c)
                act.activation(sc_sq[:, :], sc_y[:, c, :], ACT.Square)\
                    .then_inc(S["scsq_ready"], 1)

        def sc_norm_act(act, half, j, step):
            R = half * 4 + j
            for c in range(2):
                if step == SC_NORM_STEP[c]:
                    act.wait_ge(S["scn_full"], R * 2 + c + 1)
                    act.activation(sc_sq[:, :], bank(3), ACT.Ln, bias=EPS, scale=1.0 / 64)\
                        .then_inc(S["scln_ready"], 1)
                    act.wait_ge(S["scln_ready"], R * 2 + c + 1)
                    act.activation(sc_sq[:, :], sc_sq[:, :], ACT.Exp, scale=-0.5)\
                        .then_inc(S["scr_ready"], 1)
                    act.wait_ge(S["scyn_ready"], R * 2 + c + 1)
                    act.dma_start(mix_d[bass.ds(j + 4, 1), :, bass.ds(half * HALF + c * CH, CH)]
                                  .rearrange("n p t -> p (n t)"), sc_y[:, c, :])\
                        .then_inc(S["y_stored"], 16)

        def att_act(act, half, j, split_hi):
            R = half * XH + j
            act.wait_ge(S["row_full1"], (half * ROW_PASSES + R_ATT + j) * 4)
            for u in range(2):
                split_hi(nth_load(half, L_ATT + j * 2 + 1), 2 + u, u)

            def q_out(g):
                c, dt = g // 2, g % 2
                act.wait_ge(S["q_full"], R * 4 + g + 1)
                act.wait_ge(S["s_full"], R * 2)
                act.activation(qT[:, dt, c * CH:(c + 1) * CH], bank(4 + dt), ACT.Copy)\
                    .then_inc(S["q_out"], 1)

            def softmax(c):
                act.wait_ge(S["mx_ready"], R * 2 + c + 1)
                act.wait_ge(S["pt_full"], R * 2 + c)
                act.wait_ge(S["rs_ready"], R * 2 + c)
                for t in range(4):
                    act.activation(pp[:, t, :], PS[:, 6 + t // 2, (t % 2) * N_MEM:(t % 2 + 1) * N_MEM],
                                   ACT.Exp, bias=smx[:, 0, t:t + 1], scale=XD ** -0.5,
                                   accum_out=smx[:, 1, t:t + 1]).then_inc(S["p_exp"], 1)

            def pt_out(c):
                act.wait_ge(S["pt_full"], R * 2 + c + 1)
                act.wait_ge(S["pv_full"], R * 2 + c)
                act.activation(flat(pT[:, :, :]), flat(bank(4, 2)), ACT.Copy)\
                    .then_inc(S["pt_out"], 1)

            def o_hi(c):
                act.wait_ge(S["pv_full"], R * 2 + c + 1)
                act.wait_ge(S["row_full1"], (half * ROW_PASSES + R_ATT + j) * 4)
                act.activation(row_hi[:, :, c * CH:(c + 1) * CH], bank(2 * c, 2), ACT.Copy)\
                    .then_inc(S["ot_hi"], 1)

            q_out(0)
            q_out(1)
            q_out(2)
            softmax(0)
            q_out(3)
            pt_out(0)
            softmax(1)
            o_hi(0)
            pt_out(1)
            o_hi(1)
            for u in range(2):
                split_hi(nth_load(half, L_ATT + j * 2 + 2), u, u)

        def ffn_act(act, half, j, split_hi, last):
            R = half * NPAIR + j
            for f in range(2):
                if f == 1:
                    act.wait_ge(S["row_full1"], (half * ROW_PASSES + R_FFN + j) * 4)
                for u in range(2):
                    split_hi(nth_load(half, L_FFN + j * 3 + 1 + f), 2 + 2 * f + u, u)
                for c in range(2):
                    act.wait_ge(S[f"gu_full{c}"], R * 2 + f + 1)
                    act.wait_ge(S[f"ga_ready{c}"], R * 2 + f)
                    act.activation(sg[:, c, :], bank(4 + 2 * c), ACT.Silu)\
                        .then_inc(S["sg_ready"], 1)
                    act.wait_ge(S[f"ga_ready{c}"], R * 2 + f + 1)
                    act.wait_ge(S["row_full1"], (half * ROW_PASSES + R_FFN + j) * 4)
                    act.activation(row_hi[:, f, c * CH:(c + 1) * CH], aa[:, c, :], ACT.Copy)\
                        .then_inc(S["ah_ready"], 1)
            if not last:
                for u in range(2):
                    split_hi(nth_load(half, L_FFN + j * 3 + 3), u, u)

        def gates_dve(dve, half, late):
            own, sact = S["gate_step_dve"], S["gate_step_act"]
            d = half * GATE_DVE
            k = half * GATE_ACT
            count = [GD["b2"] if late else 0]

            def step(name, op, wait_act=0):
                if count[0]:
                    dve.wait_ge(own, d + count[0])
                if wait_act:
                    dve.wait_ge(sact, k + wait_act)
                op().then_inc(own, 1)
                count[0] += 1
                assert GD.get(name, count[0]) == count[0], (name, count[0])

            g = {k: v[:, :, :] for k, v in G.items()}
            if late:
                dve.wait_ge(S["gate_gc_full"], half + 1)
                step("gc", lambda: dve.tensor_copy(flat(g["gc"]), PS[:, 7, 0:TT * NH]))
                step("gl", lambda: dve.tensor_copy(flat(g["t0"]), PS[:, 7, TT * NH:2 * TT * NH]))
                step("fd", lambda: dve.tensor_tensor(g["t1"], g["t0"], g["gc"], ALU.subtract))
                step("nb", lambda: dve.tensor_tensor(g["nbeg"], g["beta"], g["egc"], ALU.mult), 6)
                step("nn", lambda: dve.tensor_scalar(g["nbeg"], g["nbeg"], -1.0, None, ALU.mult))
                assert count[0] == GATE_DVE
                return
            a_in, b_in = gate_ab[:, :, 0:NH], gate_ab[:, :, NH:2 * NH]
            dve.wait_ge(S["abt_full"], half + 1)
            dve.wait_ge(S["oo_ready"], half * TT)
            step("copy", lambda: dve.tensor_copy(
                gate_ab[:, :, :],
                bank(6, 2).rearrange("p b (t c) -> p (b t) c", t=4)[:, :, 0:2 * NH]))
            tile_bias = dtb[:, :].unsqueeze(1).broadcast_to([P, TT, NH])
            tile_nega = nega[:, :].unsqueeze(1).broadcast_to([P, TT, NH])
            step("a", lambda: dve.tensor_tensor(g["t0"], a_in, tile_bias, ALU.add))
            step("neg", lambda: dve.tensor_scalar(g["t1"], g["t0"], -1.0, None, ALU.mult))
            step("min", lambda: dve.tensor_tensor(g["t1"], g["t1"], g["t0"], ALU.min))
            step("bmin", lambda: dve.tensor_scalar(g["beta"], b_in, -1.0, 80.0, ALU.mult, ALU.min))
            step("w1", lambda: dve.tensor_scalar(g["t2"], g["t1"], 1.0, None, ALU.add), 1)
            step("wm", lambda: dve.tensor_scalar(g["t4"], g["t2"], -1.0, None, ALU.add))
            step("eq", lambda: dve.tensor_scalar(g["g"], g["t4"], 0.0, None, ALU.is_equal))
            step("mx", lambda: dve.tensor_scalar(g["t4"], g["t4"], 1e-30, None, ALU.max))
            step("rc", lambda: dve.reciprocal(g["t4"], g["t4"]))
            step("l1", lambda: dve.tensor_tensor(g["t3"], g["t3"], g["t4"], ALU.mult), 3)
            step("l2", lambda: dve.tensor_tensor(g["t3"], g["t3"], g["g"], ALU.add))
            step("l3", lambda: dve.tensor_tensor(g["t3"], g["t3"], g["t1"], ALU.mult))
            step("sp", lambda: dve.scalar_tensor_tensor(flat(g["t3"]), flat(g["t0"]), 0.0,
                                                        flat(g["t3"]), ALU.max, ALU.add))
            step("g", lambda: dve.tensor_tensor(g["g"], g["t3"], tile_nega, ALU.mult))
            step("b1", lambda: dve.tensor_scalar(g["beta"], g["beta"], 1.0, None, ALU.add), 2)
            step("b2", lambda: dve.reciprocal(g["beta"], g["beta"]))

        def conv_dve(dve, R, j, u, c, g, ci):
            b = g % 4
            dve.wait_ge(S[f"qkvz_out{b}"], CONV_OUT[g] + R * CONV_OUT_PER[b])
            dve.wait_ge(S["halo_in"], R * 3 + u + 1)
            dve.wait_ge(S["stage_ready"], R * 8 + g - 1 if g >= 2 else R * 8)
            acc = conv_acc[:, c, :]
            k = (R * 6 + g) * 3

            def tap(i):
                return cw[:, bass.ds(j, 1), u, i:i + 1].rearrange("p n k -> p (n k)")

            dve.tensor_scalar(acc, ci[:, c * CH:c * CH + CH], tap(0), None, ALU.mult)\
                .then_inc(S["conv_step"], 1)
            for i in (1, 2):
                dve.wait_ge(S["conv_step"], k + i)
                dve.scalar_tensor_tensor(acc, ci[:, c * CH + i:c * CH + i + CH], tap(i), acc,
                                         ALU.mult, ALU.add).then_inc(S["conv_step"], 1)
            dve.wait_ge(S["conv_step"], k + 3)
            dve.scalar_tensor_tensor(acc, ci[:, c * CH + 3:c * CH + 3 + CH], tap(3), acc,
                                     ALU.mult, ALU.add).then_inc(S["conv_ready"], 1)

        def gate(name, j, c):
            return over_tokens(G[name][:, bass.ds(j * 2 + c, 1), :].rearrange("p n h -> p (n h)"))

        def gdn_dve_first(dve, n, j, c):
            dve.wait_ge(S["gdn_full5"], n * 9)
            dve.tensor_tensor(ge[:, :, :], over_heads(upto[:, :]), gate("g", j, c), ALU.mult)\
                .then_inc(S["gu_ready"], 1)

        def gdn_dve(dve, half, n, c, j, step):
            if step == 0:
                dve.wait_ge(S["gdn_full6"], n * 8 + 1)
                dve.wait_ge(S["dec_ready"], n)
                dve.tensor_tensor(diff[:, :, :], r4(bank(6)), gate("gc", j, c), ALU.subtract)\
                    .then_inc(S["diff_ready"], 1)
                dve.wait_ge(S["rn_ready"], n + 1)
                dve.wait_ge(S["gdn_full6"], n * 8)
                dve.tensor_tensor(kqn[:, :, 0, :], qk[:, c, 1, :, :], rn[:, 1, :, :], ALU.mult)\
                    .then_inc(S["kqn_ready"], 1)
                dve.scalar_tensor_tensor(kqn[:, :, 1, :], qk[:, c, 0, :, :], HD ** -0.5,
                                         rn[:, 0, :, :], ALU.mult, ALU.mult)\
                    .then_inc(S["kqn_ready"], 1)
                dve.wait_ge(S["egb_ready"], n + 1)
                dve.wait_ge(S["kqn_ready"], n * 2 + 2)
                dve.tensor_tensor(ge[:, :, :], ge[:, :, :], kqn[:, :, 1, :], ALU.mult)\
                    .then_inc(S["qdec_ready"], 1)
            if step == 2:
                gram = bank(5, 2).rearrange("p b (h s t) -> p (b h) s t", h=2, s=2)
                dve.wait_ge(S["gdn_full6"], n * 8 + 2)
                dve.wait_ge(S["decm_ready"], n * 2 + 2)
                dve.tensor_tensor(dec[:, 0, :, :], gram[:, :, 0, :], dec[:, 0, :, :], ALU.mult)\
                    .then_inc(S["a_ready"], 1)
                dve.tensor_tensor(dec[:, 1, :, :], gram[:, :, 1, :], dec[:, 1, :, :], ALU.mult)\
                    .then_inc(S["attn_ready"], 1)
                dve.wait_ge(S["gdn_full4"], n * 10 + 2)
                dve.tensor_tensor(vb[:, :, :], r4(bank(4)), gate("beta", j, c), ALU.mult)\
                    .then_inc(S["vb_ready"], 1)
                dve.wait_ge(S["gdn_full7"], n * 3 + 1)
                dve.tensor_tensor(kbg[:, :, :], r4(bank(7)), gate("nbeg", j, c), ALU.mult)\
                    .then_inc(S["kbg_ready"], 1)
                dve.tensor_tensor(kdec[:, :, :], r4(bank(7)), gate("fdec", j, c), ALU.mult)\
                    .then_inc(S["kdec_ready"], 1)
            if step == 3:
                dve.wait_ge(S["gdn_full4"], n * 10 + 3)
                dve.tensor_tensor(Xm[:, :, :], over_heads(ident[:, :]), r4(bank(4)), ALU.subtract)\
                    .then_inc(S["x_ready"], 1)
            if 4 <= step < 16 and step % 2 == 1:
                l = (step - 3) // 2
                dve.wait_ge(S["gdn_full5"], n * 9 + 2 + l)
                dve.wait_ge(S["x_ready"], n * LEVELS + l)
                dve.tensor_tensor(Xm[:, :, :], Xm[:, :, :], r4(bank(5)), ALU.subtract)\
                    .then_inc(S["x_ready"], 1)
                if l < LEVELS - 1:
                    dve.wait_ge(S["gdn_full6"], n * 8 + 2 + l)
                    if l == 1:
                        dve.wait_ge(S["t1_ready"], n + 1)
                    else:
                        dve.wait_ge(S["t_ready"], n * 5 + l - 1)
                    dve.tensor_tensor(Tm[:, :, :], Tm[:, :, :], r4(bank(6)), ALU.subtract)\
                        .then_inc(S["t_ready"], 1)
            if step == 18:
                dve.wait_ge(S["gdn_full6"], n * 8 + 8)
                dve.wait_ge(S["s_ready"], n * 4)
                for hh in range(NH):
                    dve.scalar_tensor_tensor(
                        state[:, hh, :], state[:, hh, :],
                        G["elast"][:, bass.ds(j * 2 + c, 1), hh:hh + 1].rearrange("p n h -> p (n h)"),
                        r4(bank(6))[:, hh, :], ALU.mult, ALU.add).then_inc(S["s_ready"], 1)
                dve.wait_ge(S["osq_ready"], n + 1)
                dve.tensor_reduce(ost["ss"][:, :], osq[:, :, :], AX.X, ALU.add)\
                    .then_inc(S["ossum_ready"], 1)
                dve.wait_ge(S["ossum_ready"], n + 1)
                dve.tensor_scalar(ost["t"][:, :], ost["ss"][:, :], 1.0 / HD, EPS, ALU.mult, ALU.add)\
                    .then_inc(S["ost_ready"], 1)
                if c == 0:
                    gdn_dve_first(dve, n + 1, j, 1)
                k = n * 4
                dve.wait_ge(S["oy_ready"], n + 1)
                dve.tensor_tensor(ost["u"][:, :], ost["y"][:, :], ost["y"][:, :], ALU.mult)\
                    .then_inc(S["ostep"], 1)
                dve.wait_ge(S["ostep"], k + 1)
                dve.tensor_tensor(ost["v"][:, :], ost["u"][:, :], ost["t"][:, :], ALU.mult)\
                    .then_inc(S["ostep"], 1)
                dve.wait_ge(S["ostep"], k + 2)
                dve.tensor_scalar(ost["w"][:, :], ost["v"][:, :], -0.5, 1.5, ALU.mult, ALU.add)\
                    .then_inc(S["ostep"], 1)
                dve.wait_ge(S["ostep"], k + 3)
                dve.tensor_tensor(ost["r"][:, :], ost["w"][:, :], ost["y"][:, :], ALU.mult)\
                    .then_inc(S["ostep"], 1)
                dve.wait_ge(S["ostep"], k + 4)
                dve.tensor_tensor(on[:, :, :], r4(bank(5)), over_tokens(ost["r"][:, :]), ALU.mult)\
                    .then_inc(S["on_ready"], 1)
            if step == 19:
                dve.wait_ge(S["gdn_full7"], n * 3 + 3)
                dve.wait_ge(S["o_stored"], n * 16)
                dve.scalar_tensor_tensor(oo[:, :, :].rearrange("p h t -> p (h t)"), bank(7),
                                         gdng[:, 0:1], zz[:, c, :, :].rearrange("p h t -> p (h t)"),
                                         ALU.mult, ALU.mult).then_inc(S["oo_ready"], 1)

        def sc_dve(dve, half, j, g):
            R = half * 4 + j
            c = g % 2
            k = (R * 2 + c) * 3
            u = sc_u[:, 2 + c * CH:2 + (c + 1) * CH]
            if 2 <= g < 4:
                if c == 0:
                    dve.wait_ge(S["sc_halo_out"], R)
                    dve.tensor_copy(sc_u[:, 0:2], sc_halo[:, bass.ds(j, 1), :]
                                    .rearrange("p n k -> p (n k)")).then_inc(S["sc_halo_in"], 1)
                dve.wait_ge(S[f"sc_full{g % 3}"], R * 2 + g // 3 + 1)
                dve.wait_ge(S["c_out"], R * 2 + c + 1)
                dve.tensor_tensor(u, u, bank(g % 3), ALU.mult).then_inc(S["u_ready"], 1)
            if g >= 4:
                def tap(i):
                    return scw[:, bass.ds(j, 1), i:i + 1].rearrange("p n k -> p (n k)")

                dve.wait_ge(S["u_ready"], R * 2 + c + 1)
                dve.wait_ge(S["sc_halo_in"], R + 1)
                dve.wait_ge(S["scy_ready"], R * 2 + c)
                dve.tensor_scalar(sc_acc[:, :], sc_u[:, c * CH:(c + 1) * CH], tap(0), None, ALU.mult)\
                    .then_inc(S["sc_step"], 1)
                for i in (1, 2):
                    dve.wait_ge(S["sc_step"], k + i)
                    dve.scalar_tensor_tensor(sc_acc[:, :], sc_u[:, c * CH + i:c * CH + i + CH],
                                             tap(i), sc_acc[:, :], ALU.mult, ALU.add)\
                        .then_inc(S["sc_step"], 1)
                dve.wait_ge(S["sc_step"], k + 3)
                dve.wait_ge(S[f"sc_full{g % 3}"], R * 2 + g // 3 + 1)
                dve.wait_ge(S["y_stored"], R * 32)
                dve.tensor_tensor(sc_y[:, c, :], sc_acc[:, :], bank(g % 3), ALU.mult)\
                    .then_inc(S["scy_ready"], 1)
                if c == 1:
                    dve.tensor_copy(sc_halo[:, bass.ds(j, 1), :].rearrange("p n k -> p (n k)"),
                                    sc_u[:, HALF:HALF + 2]).then_inc(S["sc_halo_out"], 1)

        def sc_norm_dve(dve, half, j, step):
            R = half * 4 + j
            for c in range(2):
                if step == SC_NORM_STEP[c]:
                    dve.wait_ge(S["scr_ready"], R * 2 + c + 1)
                    dve.wait_ge(S["scy_ready"], R * 2 + c + 1)
                    dve.scalar_tensor_tensor(
                        sc_y[:, c, :], sc_y[:, c, :],
                        scg[:, bass.ds(j, 1), :].rearrange("p n k -> p (n k)"), sc_sq[:, :],
                        ALU.mult, ALU.mult).then_inc(S["scyn_ready"], 1)

        def att_dve(dve, half, j):
            R = half * XH + j

            def row_max(c):
                dve.wait_ge(S["s_full"], R * 2 + c + 1)
                dve.wait_ge(S["p_exp"], (R * 2 + c) * 4)
                dve.tensor_reduce(smx[:, 2, :],
                                  bank(6, 2).rearrange("p b (t m) -> p (b t) m", t=2), AX.X, ALU.max)\
                    .then_inc(S["mx_step"], 1)
                dve.wait_ge(S["mx_step"], R * 2 + c + 1)
                dve.tensor_scalar(smx[:, 0, :], smx[:, 2, :], -XD ** -0.5, None, ALU.mult)\
                    .then_inc(S["mx_ready"], 1)

            def scale(c):
                dve.wait_ge(S["p_exp"], (R * 2 + c + 1) * 4)
                dve.wait_ge(S["p_ready"], R * 2 + c)
                dve.reciprocal(rsum[:, :], smx[:, 1, :]).then_inc(S["rs_ready"], 1)
                dve.wait_ge(S["rs_ready"], R * 2 + c + 1)
                dve.tensor_tensor(pp[:, :, :], pp[:, :, :],
                                  rsum[:, :].unsqueeze(2).broadcast_to([P, 4, N_MEM]), ALU.mult)\
                    .then_inc(S["p_ready"], 1)

            def o_lo(c):
                dve.wait_ge(S["ot_hi"], R * 2 + c + 1)
                dve.tensor_tensor(row_lo[:, :, c * CH:(c + 1) * CH], bank(2 * c, 2),
                                  row_hi[:, :, c * CH:(c + 1) * CH].bitcast(f32), ALU.subtract)\
                    .then_inc(S["ot_lo"], 1)

            row_max(0)
            scale(0)
            row_max(1)
            scale(1)
            o_lo(0)
            o_lo(1)

        def ffn_dve(dve, half, j):
            R = half * NPAIR + j
            for f in range(2):
                for c in range(2):
                    dve.wait_ge(S["sg_ready"], R * 4 + f * 2 + c + 1)
                    dve.wait_ge(S[f"al_ready{c}"], R * 2 + f)
                    dve.tensor_tensor(aa[:, c, :], sg[:, c, :], bank(5 + 2 * c), ALU.mult)\
                        .then_inc(S[f"ga_ready{c}"], 1)

        def gdn_pe(pe, n, c, step):
            hflat = lambda t: t.rearrange("p h t -> p (h t)")
            if step == 0:
                pe.wait_ge(S["sq_ready"], n + 1)
                pe.wait_ge(S["vnew_ready"], n)
                nc.tensor.matmul(bank(4), ones[:, :], hflat(rn[:, 0, :, :]), start=True, stop=True)\
                    .then_inc(S["gdn_full4"], 1)
                pe.wait_ge(S["on_ready"], n)
                nc.tensor.matmul(bank(5), ones[:, :], hflat(rn[:, 1, :, :]), start=True, stop=True)\
                    .then_inc(S["gdn_full5"], 1)
                pe.wait_ge(S["gu_ready"], n + 1)
                pe.wait_ge(S["s_ready"], n * 4)
                nc.tensor.matmul(bank(6), ones[:, :], hflat(ge[:, :, :]), start=True, stop=True)\
                    .then_inc(S["gdn_full6"], 1)
            if step == 1:
                pe.wait_ge(S["kqn_ready"], n * 2 + 2)
                pe.wait_ge(S["oo_ready"], n)
                for hh in range(NH):
                    last = nc.tensor.transpose(r4(bank(7))[:, hh, :], kqn[:, hh, 0, :], ident[:, :])
                last.then_inc(S["gdn_full7"], 1)
                for hh in range(NH):
                    last = nc.tensor.transpose(r4(bank(4))[:, hh, :], vv[:, c, hh, :], ident[:, :])
                last.then_inc(S["gdn_full4"], 1)
            if step == 2:
                pe.wait_ge(S["egb_ready"], n + 1)
                for hh in range(NH):
                    last = nc.tensor.matmul(PS[:, 5 + hh // 2, (hh % 2) * 256:(hh % 2 + 1) * 256],
                                            kqn[:, hh, 0, :],
                                            kqn[:, hh, :, :].rearrange("p s t -> p (s t)"),
                                            start=True, stop=True)
                    if hh == 1:
                        last.then_inc(S["gdn_full5"], 1)
                last.then_inc(S["gdn_full6"], 1)
            if step == 3:
                pe.wait_ge(S["am_ready"], n * LEVELS + 1)
                pe.wait_ge(S["vb_ready"], n + 1)
                for hh in range(NH):
                    last = nc.tensor.matmul(r4(bank(4))[:, hh, :], am[:, 0, hh, :], ident[:, :],
                                            start=True, stop=True)
                last.then_inc(S["gdn_full4"], 1)
            if 4 <= step < 16 and step % 2 == 0:
                l = (step - 2) // 2
                pe.wait_ge(S["am_ready"], n * LEVELS + l + 1)
                pe.wait_ge(S["x_ready"], n * LEVELS + l)
                if l > 1:
                    pe.wait_ge(S["ym_ready"], n * 6 + l - 1)
                for hh in range(NH):
                    last = nc.tensor.matmul(r4(bank(4))[:, hh, :], am[:, l % 2, hh, :], Xm[:, hh, :],
                                            start=True, stop=True)
                last.then_inc(S["gdn_full4"], 1)
            if 4 <= step < 16 and step % 2 == 1:
                l = (step - 3) // 2
                pe.wait_ge(S["ym_ready"], n * 6 + l)
                if l == 1:
                    pe.wait_ge(S["t1_ready"], n + 1)
                    pe.wait_ge(S["attn_ready"], n + 1)
                else:
                    pe.wait_ge(S["t_ready"], n * 5 + l - 1)
                for hh in range(NH):
                    last = nc.tensor.matmul(r4(bank(5))[:, hh, :], Tm[:, hh, :], Ym[:, hh, :],
                                            start=True, stop=True)
                last.then_inc(S["gdn_full5"], 1)
                if l < LEVELS - 1:
                    for hh in range(NH):
                        last = nc.tensor.matmul(r4(bank(6))[:, hh, :], Ym[:, hh, :], Tm[:, hh, :],
                                                start=True, stop=True)
                    last.then_inc(S["gdn_full6"], 1)
            if step == 16:
                pe.wait_ge(S["x_ready"], (n + 1) * LEVELS)
                pe.wait_ge(S["kdec_ready"], n + 1)
                for hh in range(NH):
                    last = nc.tensor.matmul(r4(bank(7))[:, hh, :], kbg[:, hh, :], Xm[:, hh, :],
                                            start=True, stop=True)
                last.then_inc(S["gdn_full7"], 1)
            if step == 17:
                pe.wait_ge(S["wt_ready"], n + 1)
                pe.wait_ge(S["ym_ready"], (n + 1) * 6)
                pe.wait_ge(S["s_ready"], n * 4)
                for hh in range(NH):
                    nc.tensor.matmul(r4(bank(4))[:, hh, :], Xm[:, hh, :], vb[:, hh, :],
                                     start=True, stop=False)
                    last = nc.tensor.matmul(r4(bank(4))[:, hh, :], wt[:, hh, :], state[:, hh, :],
                                            start=False, stop=True)
                last.then_inc(S["gdn_full4"], 1)
            if step == 18:
                pe.wait_ge(S["vnew_ready"], n + 1)
                pe.wait_ge(S["qdec_ready"], n + 1)
                for hh in range(NH):
                    nc.tensor.matmul(r4(bank(5))[:, hh, :], ge[:, hh, :], state[:, hh, :],
                                     start=True, stop=False)
                    last = nc.tensor.matmul(r4(bank(5))[:, hh, :], dec[:, 1, hh, :], vnew[:, hh, :],
                                            start=False, stop=True)
                last.then_inc(S["gdn_full5"], 1)
                for hh in range(NH):
                    last = nc.tensor.matmul(r4(bank(6))[:, hh, :], kdec[:, hh, :], vnew[:, hh, :],
                                            start=True, stop=True)
                last.then_inc(S["gdn_full6"], 1)
            if step == 19:
                pe.wait_ge(S["on_ready"], n + 1)
                pe.wait_ge(S["wt_ready"], n + 1)
                for hh in range(NH):
                    last = nc.tensor.transpose(r4(bank(7))[:, hh, :], on[:, hh, :], ident[:, :])
                last.then_inc(S["gdn_full7"], 1)

        def att_pe(pe, half, j, col_slice, row_pass, norm):
            R = half * XH + j
            n_u = unit(half, U_ATT + j * 4)

            def q(c, dt):
                g = c * 2 + dt
                if c == 0:
                    pe.wait_ge(S["pt_out"], R * 2)
                else:
                    pe.wait_ge(S["q_out"], R * 4 + g - 1)
                for k in range(KT):
                    last = col_slice(PS[:, 4 + dt, :], dt, c, k)
                last.then_inc(S["q_full"], 1)

            def scores(c):
                pe.wait_ge(S["q_out"], R * 4 + 2 * c + 2)
                pe.wait_ge(S["p_exp"], (R * 2 + c) * 4)
                for t in range(4):
                    ts = slice(c * CH + t * P, c * CH + (t + 1) * P)
                    for dt in range(2):
                        last = nc.tensor.matmul(
                            PS[:, 6 + t // 2, (t % 2) * N_MEM:(t % 2 + 1) * N_MEM], qT[:, dt, ts],
                            kmem[:, bass.ds(j * 2 + dt, 1), :].rearrange("p n m -> p (n m)"),
                            start=dt == 0, stop=dt == 1)
                last.then_inc(S["s_full"], 1)

            def transposes(c):
                pe.wait_ge(S["p_ready"], R * 2 + c + 1)
                if c == 0:
                    pe.wait_ge(S["q_out"], R * 4 + 4)
                else:
                    pe.wait_ge(S["pt_out"], R * 2 + 1)
                for t in range(4):
                    for m in range(2):
                        last = nc.tensor.transpose(PS[:, 4 + m, t * P:(t + 1) * P],
                                                   pp[:, t, m * P:(m + 1) * P], ident[:, :])
                last.then_inc(S["pt_full"], 1)

            def pv(c):
                pe.wait_ge(S["pt_out"], R * 2 + c + 1)
                if c == 0:
                    pe.wait_ge(S["vh_ready"], (R + 1) * 16)
                    for par in range(2):
                        pe.wait_ge(S[f"row_out{par}"], (half * ROW_PASSES + R_ATT + j) * 4)
                for dt in range(2):
                    for m in range(2):
                        last = nc.tensor.matmul(PS[:, 2 * c + dt, :],
                                                vh[:, m, dt * P:(dt + 1) * P], pT[:, m, :],
                                                start=m == 0, stop=m == 1)
                last.then_inc(S["pv_full"], 1)

            pe.wait_ge(S["w_lo_ready"], n_u + 2)
            q(0, 0)
            q(0, 1)
            q(1, 0)
            scores(0)
            q(1, 1)
            transposes(0)
            scores(1)
            pv(0)
            transposes(1)
            pv(1)

            def ready(t):
                if t == 0:
                    pe.wait_ge(S["ot_lo"], R * 2 + 2)

            if norm is not None:
                pe.wait_ge(S["pt_out"], R * 2 + 2)
                pe.wait_ge(S["p_exp"], (R * 2 + 2) * 4)
            row_pass(half, half * ROW_PASSES + R_ATT + j, n_u + 2, [2, 3],
                     [row_hi[:, k, :] for k in (0, 1)], [row_lo[:, k, :] for k in (0, 1)],
                     ready, norm)


        block = ctx.enter_context(nc.Block())

        @block.sync
        def _(sp):
            def load_unit(n, source, slot):
                if not isinstance(n, int) or n >= 2:
                    sp.wait_ge(S["w_lo_ready"], n - 1)
                sp.dma_start(raw[slot][:, :], w_units[bass.ds(source, 1), :, :]
                             .rearrange("n p c -> p (n c)")).then_inc(S[f"raw_ready{slot}"], 16)

            def load_v(half, j):
                sp.wait_ge(S["pv_full"], (half * XH + j) * 2)
                sp.dma_start(vh[:, :, :], vmem_d[:, :, bass.ds(j * XD, XD)])\
                    .then_inc(S["vh_ready"], 16)

            def load_gain(g, before):
                sp.wait_ge(S["xn_ready"], before)
                sp.dma_start(gain[:, :], g[0:1, :].broadcast_to([P, D])).then_inc(S["gain_in"], 16)

            for dst, src in ((cw[:, :, :, :], conv_w), (scw[:, :, :], sc_w), (scg[:, :, :], sc_g),
                             (gdng[:, :], gdn_g),
                             (nega[:, :], a_log[0:1, :].broadcast_to([P, NH])),
                             (dtb[:, :], dt_bias[0:1, :].broadcast_to([P, NH]))):
                sp.dma_start(dst, src).then_inc(S["const_in"], 16)
            sp.dma_start(gain[:, :], g_mem[0:1, :].broadcast_to([P, D])).then_inc(S["gain_in"], 16)
            for t in range(2):
                sp.dma_start(xin[:, t, :], mem[t * P:(t + 1) * P, :]).then_inc(S[f"x_in{t}"], 16)
            sp.wait_ge(S["const_made"], 8)
            sp.dma_start(raw[2][:, 0:KT * 8], w_ab).then_inc(S["wab_raw"], 16)
            for n in range(MEM_UNITS):
                load_unit(n, n, n % 2)
            sp.wait_ge(S["vm_out"], 1)
            sp.dma_start(vmem_d, vmem[:, :, :]).then_inc(S["vm_stored"], 16)

            with sp.Fori(0, NHALF) as half:
                load_gain(g_mix, norm_no(half, 0, 0))
                for t in range(TT):
                    sp.wait_ge(S["xn_ready"], norm_no(half, 0, t) - (1 if t >= 2 else 0) if t >= 2
                               else norm_no(half, 0, 0))
                    sp.dma_start(xin[:, t % 2, :], x[bass.ds(half * TT + t, 1), :, :]
                                 .rearrange("n p c -> p (n c)")).then_inc(S[f"x_in{t % 2}"], 16)
                with sp.Fori(0, NH) as j:
                    for u in range(4):
                        load_unit(unit(half, U_QKVZ + j * 4 + u), MEM_UNITS + U_QKVZ + j * 4 + u, u % 2)
                load_gain(g_x, norm_no(half, 1, 0))
                with sp.Fori(0, 4) as j:
                    for u in range(3):
                        load_unit(unit(half, U_MIX + j * 3 + u), MEM_UNITS + U_MIX + j * 3 + u, u)
                for kk in range(KT):
                    load_unit(unit(half, U_OUT + kk), MEM_UNITS + U_OUT + kk, kk % 2)
                    if kk == 1:
                        sp.wait_ge(S["oo_ready"], (half + 1) * TT)
                        sp.wait_ge(S["y_stored"], (half + 1) * 16 * 8)
                        sp.wait_ge(S["o_stored"], (half + 1) * 16 * TT)
                        sp.dma_start(h[:, :, :], x[bass.ds(half * TT, TT), :, :]
                                     .rearrange("n p c -> p n c")).then_inc(S["h_in"], 16)
                with sp.Fori(0, XH - 1) as j:
                    for u in range(4):
                        load_unit(unit(half, U_ATT + j * 4 + u), MEM_UNITS + U_ATT + j * 4 + u, u % 2)
                        if u == 2:
                            load_v(half, j)
                load_gain(g_ffn, norm_no(half, 2, 0))
                for u in range(4):
                    load_unit(unit(half, U_ATT + (XH - 1) * 4 + u), MEM_UNITS + U_ATT + (XH - 1) * 4 + u, u % 2)
                    if u == 2:
                        load_v(half, XH - 1)
                with sp.Fori(0, NPAIR - 1) as j:
                    for u in range(6):
                        load_unit(unit(half, U_FFN + j * 6 + u), MEM_UNITS + U_FFN + j * 6 + u, u % 2)
                for u in range(6):
                    load_unit(unit(half, U_FFN + (NPAIR - 1) * 6 + u), MEM_UNITS + U_FFN + (NPAIR - 1) * 6 + u, u % 2)
                load_gain(g_fin, norm_no(half, 3, 0))
                for t in range(TT):
                    sp.wait_ge(S["xn_ready"], norm_no(half, 3, t) + 1)
                    sp.dma_start(out[bass.ds(half * TT + t, 1), :, :].rearrange("n p c -> p (n c)"),
                                 xn[:, t % 2, :]).then_inc(S[f"out_stored{t % 2}"], 16)
            sp.wait_ge(S["out_stored0"], NHALF * TT // 2 * 16)
            sp.wait_ge(S["out_stored1"], NHALF * TT // 2 * 16)

        @block.gpsimd
        def _(pool):
            def made():
                return S["const_made"]

            def triangle(dst, base, pattern, mult, op=ALU.is_ge):
                pool.affine_select(out=dst, in_=dst, pattern=pattern, compare_op=op, fill=0.0,
                                   base=base, channel_multiplier=mult).then_inc(made(), 1)

            pool.memset(ones[:, :], 1.0).then_inc(made(), 1)
            pool.memset(ident[:, :], 0.0).then_inc(made(), 1)
            pool.memset(group_ones[:, :], 0.0).then_inc(made(), 1)
            pool.memset(upto[:, :], 1.0).then_inc(made(), 1)
            pool.memset(level_mask[:, :, :], 0.0).then_inc(made(), 1)
            pool.memset(raw[2][:, :], 0.0).then_inc(made(), 1)
            pool.memset(halo[:, :, :, :], 0.0).then_inc(made(), 1)
            pool.memset(sc_halo[:, :, :], 0.0).then_inc(made(), 1)
            pool.memset(state[:, :, :], 0.0).then_inc(made(), 1)
            n = 9
            pool.wait_ge(made(), n)
            pool.affine_select(out=ident[:, :], in_=ident[:, :], pattern=[[-1, P]],
                               compare_op=ALU.not_equal, fill=1.0, base=0,
                               channel_multiplier=1).then_inc(made(), 1)
            triangle(upto[:, :], 0, [[1, P]], -1)
            n += 2
            for lo in (0, 64):
                pool.wait_ge(made(), n)
                pool.memset(group_ones[lo:lo + 64, lo:lo + 64], 1.0).then_inc(made(), 1)
                n += 1
            for l in range(LEVELS):
                b = 1 << l
                m = P // (2 * b)
                v = level_mask[:, l, :].rearrange("p (m e c) -> p m e c", e=2, c=b)[:, :, 0, :]
                pool.wait_ge(made(), n)
                pool.memset(v, 1.0).then_inc(made(), 1)
                n += 1
                pool.wait_ge(made(), n)
                triangle(v, -b, [[-2 * b, m], [0, b]], 1)
                n += 1
                pool.wait_ge(made(), n)
                triangle(v, 2 * b - 1, [[2 * b, m], [0, b]], -1)
                n += 1
            assert n == CONSTS

            def split_lo(n):
                number, slot, raw_slot = n
                pool.wait_ge(S["w_hi_ready"], number + 1)
                pool.tensor_tensor(w_lo[slot][:, :], raw[raw_slot][:, :],
                                   w_hi[slot][:, :].bitcast(f32), ALU.subtract)\
                    .then_inc(S["w_lo_ready"], 1)

            pool.wait_ge(S["wab_hi_ready"], 1)
            pool.tensor_tensor(wab_lo[:, :], raw[2][:, 0:KT * 8 + P], wab_hi[:, :].bitcast(f32),
                               ALU.subtract).then_inc(S["wab_lo_ready"], 1)
            for n in range(MEM_UNITS):
                split_lo((n, n % RING, n % 2))

            with pool.Fori(0, NHALF) as half:
                for u in range(2):
                    split_lo((unit(half, U_QKVZ + u), u, u))
                with pool.Fori(0, NH) as j:
                    for u in range(4):
                        split_lo((unit(half, U_QKVZ + j * 4 + u + 2), (u + 2) % 4, u % 2))

                with pool.Fori(0, 4) as j:
                    n_u = unit(half, U_MIX + j * 3)
                    split_lo((n_u + 2, 2, 2))
                    for c in range(2):
                        n = half * TT + j * 2 + c
                        for step in range(STEPS):
                            gdn_pool(pool, n, c, j, step)
                            for g in groups_after(c * STEPS + step):
                                if g == 1:
                                    split_lo((n_u + 3, 0, 0))
                                if g == 3:
                                    split_lo((n_u + 4, 1, 1))
                for i in range(KT // 2):
                    for k in range(2):
                        hi = w_hi[4 + k][:, :] if i % 2 == 0 else row_hi[:, k, :]
                        lo = w_lo[4 + k][:, :] if i % 2 == 0 else row_lo[:, k, :]
                        pool.wait_ge(S["mix_hi_ready"], half * KT + 2 * i + k + 1)
                        pool.tensor_tensor(lo, mixraw[:, k, :], hi.bitcast(f32), ALU.subtract)\
                            .then_inc(S["mix_lo_ready"], 1)
                    for k in range(2):
                        split_lo((unit(half, U_OUT + 2 * i + k + 2), (2 * i + k + 2) % 4, k))
                with pool.Fori(0, XH) as j:
                    for u in range(4):
                        split_lo((unit(half, U_ATT + j * 4 + u + 2), (u + 2) % 4, u % 2))
                with pool.Fori(0, NPAIR - 1) as j:
                    ffn_pool(pool, half, j, split_lo, False)
                ffn_pool(pool, half, NPAIR - 1, split_lo, True)

        @block.scalar
        def _(act):
            def split_hi(load, slot, raw_slot):
                act.wait_ge(S[f"raw_ready{raw_slot}"], 16 * load)
                act.activation(w_hi[slot][:, :], raw[raw_slot][:, :], ACT.Copy)\
                    .then_inc(S["w_hi_ready"], 1)

            def norm_stats(src, par, no, ready):
                ready(act)
                act.activation(xn[:, par, :], src, ACT.Square, accum_out=stat["ss"][:, par:par + 1])\
                    .then_inc(S["ss_ready"], 1)
                act.wait_ge(S["ss_ready"], no + 1)
                act.activation(stat["l"][:, par:par + 1], stat["ss"][:, par:par + 1], ACT.Ln,
                               bias=EPS, scale=1.0 / D).then_inc(S["ln_ready"], 1)
                act.wait_ge(S["ln_ready"], no + 1)
                act.activation(stat["y"][:, par:par + 1], stat["l"][:, par:par + 1], ACT.Exp,
                               scale=-0.5).then_inc(S["y_ready"], 1)

            def norm_hi(t, count, dst=None):
                act.wait_ge(S[f"tr_full{t % 2}"], count + 1)
                act.activation(act_hi[:, :, t * P:(t + 1) * P],
                               bank(4 + 2 * (t % 2), 2).rearrange("p b (k t) -> p (b k) t", k=4),
                               ACT.Copy).then_inc(S["tr_hi"], 1)

            def norm_act(half, which, src, ready, transposes):
                for s in range(TT + 2):
                    if s >= 2 and transposes:
                        norm_hi(s - 2, transposed(half, which) + (s - 2) // 2)
                    if s < TT:
                        par = s % 2
                        act.wait_ge(S[f"tr_full{par}"], transposed(half, which)
                                    + (s // 2 if transposes else 0))
                        act.wait_ge(S[f"out_stored{par}"],
                                    16 * (half * (TT // 2) + (0 if transposes else s // 2)))
                        norm_stats(src(s), par, norm_no(half, which, s), ready(s))

            act.preload_act_table_set("natural_log_exp_and_others")
            act.wait_ge(S["const_in"], 6 * 16)
            act.activation(nega[:, :], nega[:, :], ACT.Exp).then_inc(S["nega_ready"], 1)
            act.wait_ge(S["nega_ready"], 1)
            act.activation(nega[:, :], nega[:, :], ACT.Copy, scale=-1.0)\
                .then_inc(S["nega_ready"], 1)
            act.wait_ge(S["wab_raw"], 16)
            act.activation(wab_hi[:, :], raw[2][:, 0:KT * 8 + P], ACT.Copy)\
                .then_inc(S["wab_hi_ready"], 1)
            for t in range(2):
                norm_stats(xin[:, t, :], t, t,
                           lambda e, t=t: e.wait_ge(S[f"x_in{t}"], 16))
            for t in range(2):
                norm_hi(t, 0)
            for n in range(MEM_UNITS):
                if RING <= n < RING + KT:
                    act.wait_ge(S[f"km_full{n % 2}"], (n - RING) // 2 + 1)
                elif n >= RING + KT:
                    act.wait_ge(S["vm_full"], n - RING - KT + 1)
                split_hi(n // 2 + 1, n % RING, n % 2)
            act.wait_ge(S["vm_full"], KT)
            act.activation(flat(vmem[:, :, :]), flat(bank(4, 4)), ACT.Copy)\
                .then_inc(S["vm_out"], 1)

            with act.Fori(0, NHALF) as half:
                act.preload_act_table_set("natural_log_exp_and_others")
                norm_act(half, 0, lambda t: xin[:, t % 2, :],
                         lambda t: (lambda e: e.wait_ge(
                             S[f"x_in{t % 2}"], 16 * (1 + half * (TT // 2) + t // 2 + 1))), True)
                for u in range(2):
                    split_hi(nth_load(half, L_QKVZ), u, u)
                act.wait_ge(S["vm_stored"], 16)
                for c in range(NCH):
                    act.wait_ge(S[f"ab_full{c}"], half + 1)
                    act.activation(ab_t[:, c * CH:(c + 1) * CH], PS[:, c, :], ACT.Copy)\
                        .then_inc(S["ab_out"], 1)
                gates_act(act, half)

                act.preload_act_table_set("silu_and_others")
                with act.Fori(0, NH) as j:
                    R = half * NH + j
                    for u in range(4):
                        split_hi(nth_load(half, L_QKVZ + j * 2 + u // 2 + 1), (u + 2) % 4, u % 2)
                        for c in range(NCH):
                            g = u * 2 + c
                            b = g % 4
                            if u < 3:
                                if c == 0:
                                    act.wait_ge(S["halo_out"], 3 * R + u - 1 if u >= 2
                                                else 3 * R)
                                act.wait_ge(S[f"qkvz_full{b}"], R * 2 + g // 4 + 1)
                                act.activation(conv_in[u % 2][:, 3 + c * CH:3 + (c + 1) * CH],
                                               bank(b), ACT.Copy).then_inc(S[f"qkvz_out{b}"], 1)
                                if g > 0:
                                    silu_store(act, half, j, R, g - 1)
                            else:
                                if c == 0:
                                    silu_store(act, half, j, R, g - 1)
                                silu_z(act, half, j, R, g)
                act.preload_act_table_set("natural_log_exp_and_others")
                gates_act_late(act, half)

                act.wait_ge(S["halo_out"], (half + 1) * NH * 3)
                act.wait_ge(S["st_stored0"], (half + 1) * NH * 4 * 16)
                act.wait_ge(S["st_stored1"], (half + 1) * NH * 4 * 16)
                with act.Fori(0, 4) as j:
                    for c in range(2):
                        load_chunk(act, half, half * TT + j * 2 + c, j * 2 + c, c)
                    split_hi(half * 4 + j + 1, 2, 2)
                    for c in range(2):
                        n = half * TT + j * 2 + c
                        if c == 0:
                            gdn_act_first(act, n, c)
                        for step in range(STEPS):
                            gdn_act(act, half, n, c, j, step)
                            for g in groups_after(c * STEPS + step):
                                sc_act(act, half, j, g)
                                if g == 1:
                                    split_hi(nth_load(half, L_MIX + j + 1), 0, 0)
                                if g == 3:
                                    act.wait_ge(S["sc_full0"], (half * 4 + j) * 2 + 2)
                                    split_hi(nth_load(half, L_MIX + j + 1), 1, 1)
                            sc_norm_act(act, half, j, c * STEPS + step)

                act.wait_ge(S["oo_ready"], (half + 1) * TT)
                act.wait_ge(S["y_stored"], (half + 1) * 16 * 8)
                act.wait_ge(S["o_stored"], (half + 1) * 16 * TT)
                for k in range(2):
                    load_mix(act, half, k)
                for i in range(KT // 2):
                    for k in range(2):
                        kk = 2 * i + k
                        slot = w_hi[4 + k][:, :] if i % 2 == 0 else row_hi[:, k, :]
                        act.wait_ge(S[f"mix_in{k}"], (half * KT // 2 + i + 1) * 16)
                        act.activation(slot, mixraw[:, k, :], ACT.Copy)\
                            .then_inc(S["mix_hi_ready"], 1)
                    act.wait_ge(S["row_full1"], (half * ROW_PASSES + i) * 4)
                    for k in range(2):
                        split_hi(nth_load(half, L_OUT + i + 1), (2 * i + k + 2) % 4, k)
                    if i < KT // 2 - 1:
                        for k in range(2):
                            act.wait_ge(S["mix_lo_ready"], half * KT + 2 * i + k + 1)
                            load_mix(act, half, 2 * i + 2 + k)
                act.wait_ge(S["mix_lo_ready"], (half + 1) * KT)
                norm_act(half, 1, lambda t: h[:, t, :],
                         lambda t: (lambda e: e.wait_ge(
                             S[f"row_out{t % 2}"],
                             (half * ROW_PASSES + R_OUT + KT // 2 - 1) * 4 + t // 2 + 1)), True)

                with act.Fori(0, XH - 1) as j:
                    att_act(act, half, j, split_hi)
                att_act(act, half, XH - 1, split_hi)
                norm_act(half, 2, lambda t: h[:, t, :],
                         lambda t: (lambda e: e.wait_ge(
                             S[f"row_out{t % 2}"],
                             (half * ROW_PASSES + R_ATT + XH - 1) * 4 + t // 2 + 1)), True)

                act.preload_act_table_set("silu_and_others")
                with act.Fori(0, NPAIR - 1) as j:
                    ffn_act(act, half, j, split_hi, False)
                ffn_act(act, half, NPAIR - 1, split_hi, True)
                act.preload_act_table_set("natural_log_exp_and_others")
                for c in range(2):
                    act.wait_ge(S[f"al_ready{c}"], (half + 1) * NPAIR * 2)
                norm_act(half, 3, lambda t: h[:, t, :],
                         lambda t: (lambda e: e.wait_ge(
                             S[f"row_out{t % 2}"],
                             (half * ROW_PASSES + ROW_PASSES - 1) * 4 + t // 2 + 1)), False)

        @block.vector
        def _(dve):
            def norm_tile(src, par, no, first=None):
                if first:
                    first()
                """xn = src * rstd * gain, rstd by one Newton step from ScalarE's estimate."""
                col = {k: v[:, par:par + 1] for k, v in stat.items()}
                own = S["nstat"]
                dve.wait_ge(S["ss_ready"], no + 1)
                dve.tensor_scalar(col["t"], col["ss"], 1.0 / D, EPS, ALU.mult, ALU.add)\
                    .then_inc(own, 1)
                dve.wait_ge(S["y_ready"], no + 1)
                dve.wait_ge(own, no * 4 + 1)
                dve.scalar_tensor_tensor(col["u"], col["t"], col["y"], col["y"], ALU.mult, ALU.mult)\
                    .then_inc(own, 1)
                dve.wait_ge(own, no * 4 + 2)
                dve.tensor_scalar(col["v"], col["u"], -0.5, 1.5, ALU.mult, ALU.add)\
                    .then_inc(own, 1)
                dve.wait_ge(own, no * 4 + 3)
                dve.tensor_tensor(col["r"], col["v"], col["y"], ALU.mult).then_inc(own, 1)
                dve.wait_ge(own, no * 4 + 4)
                dve.scalar_tensor_tensor(xn[:, par, :], src, col["r"], gain[:, :],
                                         ALU.mult, ALU.mult).then_inc(S["xn_ready"], 1)

            def norm_lo(t, hi_count):
                dve.wait_ge(S["tr_hi"], hi_count + 1)
                dve.tensor_tensor(act_lo[:, :, t * P:(t + 1) * P],
                                  bank(4 + 2 * (t % 2), 2).rearrange("p b (k t) -> p (b k) t", k=4),
                                  act_hi[:, :, t * P:(t + 1) * P].bitcast(f32), ALU.subtract)\
                    .then_inc(S[f"tr_lo{t % 2}"], 1)

            def row_add(t, rp):
                dve.wait_ge(S[f"row_full{t % 2}"], rp * 4 + t // 2 + 1)
                dve.wait_ge(S[f"row_out{t % 2}"], rp * 4)
                dve.tensor_tensor(h[:, t, :], h[:, t, :], flat(bank(2 * (t % 2), 2)), ALU.add)\
                    .then_inc(S[f"row_out{t % 2}"], 1)

            def norm_dve(half, which, src, rp, transposes):
                for s in range(TT + 2):
                    if s < TT and rp is not None:
                        row_add(s, rp)
                    if 1 <= s <= TT:
                        norm_tile(src(s - 1), (s - 1) % 2, norm_no(half, which, s - 1))
                    if s >= 2 and transposes:
                        norm_lo(s - 2, 2 + (half * 3 + which) * TT + s - 2)

            dve.wait_ge(S["gain_in"], 16)
            for t in range(2):
                norm_tile(xin[:, t, :], t, t)
            for t in range(2):
                norm_lo(t, t)
            for u in range(KT):
                b = u % 2
                dve.wait_ge(S[f"km_full{b}"], u // 2 + 1)
                dve.tensor_copy(kmem[:, u, :], PS[:, b, 0:N_MEM]).then_inc(S[f"km_out{b}"], 1)
            dve.wait_ge(S["const_made"], CONSTS)

            with dve.Fori(0, NHALF) as half:
                dve.wait_ge(S["gain_in"], (half * 4 + 2) * 16)
                norm_dve(half, 0, lambda t: xin[:, t % 2, :], None, True)
                gates_dve(dve, half, False)
                with dve.Fori(0, NH) as j:
                    R = half * NH + j
                    for u in range(3):
                        ci = conv_in[u % 2]
                        dve.wait_ge(S["halo_out"], 3 * R + u - 1 if u >= 2 else 3 * R)
                        dve.tensor_copy(ci[:, 0:3], halo[:, bass.ds(j, 1), u, :]
                                        .rearrange("p n k -> p (n k)")).then_inc(S["halo_in"], 1)
                        for c in range(NCH):
                            g = u * 2 + c
                            conv_dve(dve, R, j, u, c, g, ci)
                        dve.tensor_copy(halo[:, bass.ds(j, 1), u, :]
                                        .rearrange("p n k -> p (n k)"), ci[:, HALF:HALF + 3])\
                            .then_inc(S["halo_out"], 1)
                gates_dve(dve, half, True)
                with dve.Fori(0, 4) as j:
                    for c in range(2):
                        n = half * TT + j * 2 + c
                        if c == 0:
                            gdn_dve_first(dve, n, j, c)
                        for step in range(STEPS):
                            gdn_dve(dve, half, n, c, j, step)
                            for g in groups_after(c * STEPS + step):
                                sc_dve(dve, half, j, g)
                            sc_norm_dve(dve, half, j, c * STEPS + step)
                dve.wait_ge(S["h_in"], (half + 1) * 16)
                for i in range(KT // 2 - 1):
                    for t in range(TT):
                        row_add(t, half * ROW_PASSES + i)
                dve.wait_ge(S["gain_in"], (half * 4 + 3) * 16)
                norm_dve(half, 1, lambda t: h[:, t, :], half * ROW_PASSES + KT // 2 - 1, True)
                with dve.Fori(0, XH - 1) as j:
                    att_dve(dve, half, j)
                    for t in range(TT):
                        row_add(t, half * ROW_PASSES + R_ATT + j)
                att_dve(dve, half, XH - 1)
                dve.wait_ge(S["gain_in"], (half * 4 + 4) * 16)
                norm_dve(half, 2, lambda t: h[:, t, :], half * ROW_PASSES + R_ATT + XH - 1, True)
                with dve.Fori(0, NPAIR - 1) as j:
                    ffn_dve(dve, half, j)
                    for t in range(TT):
                        row_add(t, half * ROW_PASSES + R_FFN + j)
                ffn_dve(dve, half, NPAIR - 1)
                dve.wait_ge(S["gain_in"], (half * 4 + 5) * 16)
                norm_dve(half, 3, lambda t: h[:, t, :], half * ROW_PASSES + ROW_PASSES - 1, False)

        @block.tensor
        def _(pe):
            def three(out_ap, whi, wlo, xhi, xlo, start, stop):
                nc.tensor.matmul(out_ap, whi, xhi, start=start, stop=False)
                nc.tensor.matmul(out_ap, whi, xlo, start=False, stop=False)
                return nc.tensor.matmul(out_ap, wlo, xhi, start=False, stop=stop)

            def col_slice(out_ap, slot, c, k, width=CH):
                ks = slice(k * P, (k + 1) * P)
                cs = slice(c * CH, c * CH + width)
                return three(out_ap, w_hi[slot][:, ks], w_lo[slot][:, ks],
                             act_hi[:, k, cs], act_lo[:, k, cs], k == 0, k == KT - 1)

            def transpose_tile(t, count, xn_count):
                pe.wait_ge(S["xn_ready"], xn_count + 1)
                pe.wait_ge(S[f"tr_lo{t % 2}"], count)
                for k in range(KT):
                    last = nc.tensor.transpose(PS[:, 4 + 2 * (t % 2) + k // 4,
                                                  (k % 4) * P:(k % 4 + 1) * P],
                                               xn[:, t % 2, k * P:(k + 1) * P], ident[:, :])
                last.then_inc(S[f"tr_full{t % 2}"], 1)

            def row_pass(half, rp, n_u, slots, a_hi, a_lo, ready, norm=None):
                pe.wait_ge(S["w_lo_ready"], n_u + 2)
                for s in range(TT + 2):
                    if s < TT:
                        t = s
                        ready(t)
                        pe.wait_ge(S[f"row_out{t % 2}"], rp * 4 + t // 2)
                        for nh in range(2):
                            ts = slice(t * P, (t + 1) * P)
                            ns = slice(nh * CH, (nh + 1) * CH)
                            out_ap = PS[:, 2 * (t % 2) + nh, :]
                            for i in range(2):
                                nc.tensor.matmul(out_ap, a_hi[i][:, ts], w_hi[slots[i]][:, ns],
                                                 start=i == 0, stop=False)
                                nc.tensor.matmul(out_ap, a_hi[i][:, ts], w_lo[slots[i]][:, ns],
                                                 start=False, stop=False)
                                last = nc.tensor.matmul(out_ap, a_lo[i][:, ts],
                                                        w_hi[slots[i]][:, ns],
                                                        start=False, stop=i == 1)
                        last.then_inc(S[f"row_full{t % 2}"], 1)
                    if norm is not None and s >= 2:
                        transpose_tile(s - 2, transposed(half, norm) + (s - 2) // 2,
                                       norm_no(half, norm, s - 2))

            pe.wait_ge(S["const_made"], CONSTS)
            for t in range(2):
                transpose_tile(t, 0, t)
            for t in range(2):
                pe.wait_ge(S[f"tr_lo{t}"], 1)
            for u in range(KT):
                b = u % 2
                pe.wait_ge(S["w_lo_ready"], u + 1)
                pe.wait_ge(S[f"km_out{b}"], u // 2)
                for k in range(KT):
                    last = col_slice(PS[:, b, 0:N_MEM], u % RING, 0, k, N_MEM)
                last.then_inc(S[f"km_full{b}"], 1)
            for k in range(KT):
                n = KT + k
                pe.wait_ge(S["w_lo_ready"], n + 1)
                for m in range(2):
                    for nh in range(2):
                        ms = slice(m * P, (m + 1) * P)
                        ns = slice(nh * CH, (nh + 1) * CH)
                        last = three(PS[:, 4 + 2 * m + nh, :], act_hi[:, k, ms], act_lo[:, k, ms],
                                     w_hi[n % RING][:, ns], w_lo[n % RING][:, ns],
                                     k == 0, k == KT - 1)
                last.then_inc(S["vm_full"], 1)
            pe.wait_ge(S["vm_out"], 1)

            with pe.Fori(0, NHALF) as half:
                for c in range(2):
                    pe.wait_ge(S[f"ga_ready{c}"], half * NPAIR * 2)
                for t in range(TT):
                    transpose_tile(t, transposed(half, 0) + t // 2, norm_no(half, 0, t))
                for par in range(2):
                    pe.wait_ge(S[f"tr_lo{par}"], transposed(half, 1))
                for par in range(2):
                    pe.wait_ge(S[f"row_out{par}"], half * ROW_PASSES * 4)
                for b in range(2):
                    pe.wait_ge(S[f"km_out{b}"], KT // 2)
                pe.wait_ge(S["wab_lo_ready"], 1)
                for c in range(NCH):
                    for k in range(KT):
                        ks = slice(k * 8, k * 8 + P)
                        cs = slice(c * CH, (c + 1) * CH)
                        last = three(PS[:, c, :], wab_hi[:, ks], wab_lo[:, ks],
                                     act_hi[:, k, cs], act_lo[:, k, cs], k == 0, k == KT - 1)
                    last.then_inc(S[f"ab_full{c}"], 1)
                pe.wait_ge(S["ab_out"], (half + 1) * 2)
                for t in range(TT):
                    last = nc.tensor.transpose(PS[:, 6 + t // 4, t % 4 * P:(t % 4 + 1) * P],
                                               ab_t[:, t * P:(t + 1) * P], ident[:, :])
                last.then_inc(S["abt_full"], 1)

                with pe.Fori(0, NH) as j:
                    R = half * NH + j
                    for u in range(4):
                        n = unit(half, U_QKVZ + j * 4 + u)
                        pe.wait_ge(S["w_lo_ready"], n + 1)
                        for c in range(NCH):
                            g = u * 2 + c
                            b = g % 4
                            if g >= 4:
                                pe.wait_ge(S[f"qkvz_out{b}"], CONV_OUT[g - 4] + R * CONV_OUT_PER[b])
                            else:
                                pe.wait_ge(S["stage_ready"], R * 8)
                                pe.wait_ge(S[f"qkvz_out{b}"], R * CONV_OUT_PER[b])
                            for k in range(KT):
                                last = col_slice(PS[:, b, :], u, c, k)
                            last.then_inc(S[f"qkvz_full{b}"], 1)
                pe.wait_ge(S["stage_ready"], (half + 1) * NH * 8)

                for b in range(4):
                    pe.wait_ge(S[f"qkvz_out{b}"], (half + 1) * NH * CONV_OUT_PER[b])
                pe.wait_ge(S["gate_step_dve"], half * GATE_DVE + GD["g"])
                nc.tensor.matmul(PS[:, 7, 0:TT * NH], upto[:, :], flat(G["g"][:, :, :]),
                                 start=True, stop=True)
                nc.tensor.matmul(PS[:, 7, TT * NH:2 * TT * NH], ones[:, :], flat(G["g"][:, :, :]),
                                 start=True, stop=True).then_inc(S["gate_gc_full"], 1)

                with pe.Fori(0, 4) as j:
                    pe.wait_ge(S["gate_step_dve"], half * GATE_DVE + GD["gl"])
                    R = half * 4 + j
                    n_u = unit(half, U_MIX + j * 3)

                    def sc_slices(a, b):
                        for s in range(a, b):
                            u, c, k = s // (NCH * KT), s // KT % NCH, s % KT
                            g = u * 2 + c
                            if k == 0:
                                if c == 0:
                                    pe.wait_ge(S["w_lo_ready"], n_u + u + 1)
                                if g <= 2:
                                    pe.wait_ge(S["scy_ready"], R * 2)
                                if g == 3 or g == 4:
                                    pe.wait_ge(S["c_out"], R * 2 + g - 2)
                                if g == 5:
                                    pe.wait_ge(S["u_ready"], R * 2 + 1)
                            last = col_slice(PS[:, g % 3, :], u, c, k)
                            if k == KT - 1:
                                last.then_inc(S[f"sc_full{g % 3}"], 1)

                    sc_slices(0, slices_before(0))
                    for c in range(2):
                        n = half * TT + j * 2 + c
                        for step in range(STEPS):
                            at = c * STEPS + step
                            gdn_pe(pe, n, c, step)
                            sc_slices(slices_before(at), slices_before(at + 1))
                            for cc in range(2):
                                if at == SC_NORM_STEP[cc]:
                                    pe.wait_ge(S["scsq_ready"], R * 2 + cc + 1)
                                    pe.wait_ge(S["scln_ready"], R * 2 + cc)
                                    nc.tensor.matmul(PS[:, 3, :], group_ones[:, :], sc_sq[:, :],
                                                     start=True, stop=True)\
                                        .then_inc(S["scn_full"], 1)

                pe.wait_ge(S["scyn_ready"], (half + 1) * 8)
                for i in range(KT // 2):
                    even = i % 2 == 0
                    hi = [w_hi[4][:, :], w_hi[5][:, :]] if even else [row_hi[:, k, :] for k in (0, 1)]
                    lo = [w_lo[4][:, :], w_lo[5][:, :]] if even else [row_lo[:, k, :] for k in (0, 1)]
                    final = i == KT // 2 - 1
                    n_u = unit(half, U_OUT + 2 * i)

                    def ready(t, i=i):
                        if t == 0:
                            pe.wait_ge(S["mix_lo_ready"], half * KT + 2 * i + 2)

                    if final:
                        pe.wait_ge(S["oo_ready"], (half + 1) * TT)
                        pe.wait_ge(S["s_ready"], (half + 1) * TT * 4)
                    row_pass(half, half * ROW_PASSES + i, n_u, [2 * i % 4, 2 * i % 4 + 1], hi, lo,
                             ready, 1 if final else None)

                with pe.Fori(0, XH - 1) as j:
                    for par in range(2):
                        pe.wait_ge(S[f"tr_lo{par}"], transposed(half, 2))
                    att_pe(pe, half, j, col_slice, row_pass, None)
                att_pe(pe, half, XH - 1, col_slice, row_pass, 2)

                with pe.Fori(0, NPAIR) as j:
                    for par in range(2):
                        pe.wait_ge(S[f"tr_lo{par}"], transposed(half, 3))
                    R = half * NPAIR + j
                    n_u = unit(half, U_FFN + j * 6)
                    for f in range(2):
                        pe.wait_ge(S["w_lo_ready"], n_u + 2 * f + 2)
                        for c in range(2):
                            pe.wait_ge(S[f"ga_ready{c}"], R * 2 + f)
                            for k in range(KT):
                                col_slice(PS[:, 4 + 2 * c, :], 2 * f, c, k)
                            for k in range(KT):
                                last = col_slice(PS[:, 5 + 2 * c, :], 2 * f + 1, c, k)
                            last.then_inc(S[f"gu_full{c}"], 1)

                    def ready(t):
                        if t % 4 == 0:
                            pe.wait_ge(S[f"al_ready{t // 4}"], R * 2 + 2)

                    row_pass(half, half * ROW_PASSES + R_FFN + j, n_u + 4, [4, 5],
                             [row_hi[:, k, :] for k in (0, 1)], [row_lo[:, k, :] for k in (0, 1)],
                             ready)

_VECTORS = {"g_mix": "norm_mix_g", "g_mem": "norm_mem_g", "g_x": "norm_x_g",
            "g_ffn": "norm_ffn_g", "g_fin": "norm_final_g"}


def _units(inputs):
    import numpy as np

    def columns(w, first, count):
        w = w[:, first:first + count * P].reshape(KT, P, count, P)
        return w.transpose(2, 1, 0, 3).reshape(count, P, D)

    def rows(w):
        return w.reshape(-1, P, D)

    w = {k: np.asarray(inputs[k])[0] for k in
         ("w_in", "w_out", "w_xq", "w_xk", "w_xv", "w_xo", "w_gate", "w_up", "w_down")}
    width = NH * HD
    q, k, v, z = (columns(w["w_in"], i * width, NH) for i in range(4))
    first = 4 * width + 2 * NH
    b, c, hh = (columns(w["w_in"], first + i * width, 4) for i in range(3))
    wo = rows(w["w_out"])
    xq, xo = columns(w["w_xq"], 0, KT), rows(w["w_xo"])
    gate, up, down = columns(w["w_gate"], 0, FF // P), columns(w["w_up"], 0, FF // P), rows(w["w_down"])
    parts = [columns(w["w_xk"], 0, KT), rows(w["w_xv"])]
    parts += [np.stack([q, k, v, z], 1).reshape(-1, P, D)]
    parts += [np.stack([c, hh, b], 1).reshape(-1, P, D)]
    parts += [np.concatenate([wo[4:], wo[:4]])]
    parts += [np.concatenate([xq.reshape(XH, 2, P, D), xo.reshape(XH, 2, P, D)], 1)
              .reshape(-1, P, D)]
    parts += [np.concatenate([np.stack([gate, up], 1).reshape(NPAIR, 4, P, D),
                              down.reshape(NPAIR, 2, P, D)], 1).reshape(-1, P, D)]
    units = np.concatenate(parts)
    ab = w["w_in"][:, 4 * width:first].reshape(KT, P, 2 * NH).transpose(1, 0, 2).reshape(P, -1)
    return units, ab


def kernel(**inputs):
    import numpy as np
    import concourse.bacc as bacc
    from concourse.bass_utils import run_bass_kernel_spmd

    a = {k: np.asarray(v) for k, v in inputs.items()}
    units, ab = _units(a)
    arrays = {
        "x": a["x"].reshape(SEQ // P, P, D),
        "mem": a["mem"].reshape(N_MEM, D),
        "w_units": units,
        "w_ab": ab,
        "conv_w": a["conv_qkv_w"][0].reshape(4, 3, NH, P).transpose(3, 2, 1, 0),
        "sc_w": a["conv_sc_w"][0].reshape(3, 4, P).transpose(2, 1, 0),
        "a_log": a["a_log"].reshape(1, NH),
        "dt_bias": a["dt_bias"].reshape(1, NH),
        "gdn_g": a["gdn_norm_g"].reshape(P, 1),
        "sc_g": a["sc_norm_g"].reshape(4, P, 1).transpose(1, 0, 2),
    }
    for name, source in _VECTORS.items():
        arrays[name] = a[source].reshape(1, D)
    arrays = {k: np.ascontiguousarray(v) for k, v in arrays.items()}
    nc = bacc.Bacc("TRN2", target_bir_lowering=False, num_devices=1)
    aps = {k: nc.dram_tensor("in_" + k, v.shape, mybir.dt.from_np(v.dtype),
                             kind="ExternalInput").ap() for k, v in arrays.items()}
    out = nc.dram_tensor("out", (SEQ // P, P, D), f32, kind="ExternalOutput").ap()
    block_kernel(nc, out=out, **aps)
    r = run_bass_kernel_spmd(nc, [{"in_" + k: v for k, v in arrays.items()}], core_ids=[0])
    return r.results[0]["out"].reshape(1, SEQ, D)
```

```python
import concourse.bass as bass
from concourse import mybir
from contextlib import ExitStack

f32 = mybir.dt.float32
f32r = mybir.dt.float32r
ACT = mybir.ActivationFunctionType
ALU = mybir.AluOpType
AX = mybir.AxisListType

P = 128
SEQ = 2048
D = 1024
KT = D // P
HALF = 1024
NHALF = SEQ // HALF
TT = HALF // P
CH = 512
NCH = HALF // CH
NH = 4
HD = 128
N_MEM = 256
XH = 4
XD = D // XH
FF = 2816
NPAIR = FF // (2 * P)
EPS = 1e-6
LEVELS = 7

MEM_UNITS = 2 * KT
QKVZ_UNITS = 4 * NH
MIX_UNITS = 3 * 4
OUT_UNITS = KT
ATT_UNITS = 4 * XH
FFN_UNITS = 6 * NPAIR
HALF_UNITS = QKVZ_UNITS + MIX_UNITS + OUT_UNITS + ATT_UNITS + FFN_UNITS
RING = 4
CONSTS = 35
GD = {n: i + 1 for i, n in enumerate(
    "copy a neg min bmin w1 wm eq mx rc l1 l2 l3 sp g b1 b2 gc gl fd nb nn".split())}
GATE_DVE = len(GD)
GATE_ACT = 6
CONV_OUT = [1 + g // 4 for g in range(6)]
CONV_OUT_PER = [2, 2, 1, 1]
ROW_PASSES = KT // 2 + XH + NPAIR

STEPS = ["load", "start", "gram", "a1t"] + [f"{x}{l}" for l in range(1, LEVELS) for x in "yx"] + list("wvo")
FILL_LEVELS = [1, 1] * 6
FILL = [0, 0, 4, 3] + FILL_LEVELS + [2, 2, 1]
FILL_FIRST = [5, 3, 0, 0] + FILL_LEVELS + [2, 1, 1]
CHUNK_SLICES = 3 * NCH * KT // 2
assert sum(FILL) == sum(FILL_FIRST) == CHUNK_SLICES


def block_kernel(nc, x, mem, w_units, w_ab, conv_w, sc_w, a_log, dt_bias, gdn_g, sc_g,
                 g_mix, g_mem, g_x, g_ffn, g_fin, out):
    ctx = ExitStack()
    with ctx:
        cursor = [16512]

        def sb(name, shape, dt=f32, at=None):
            size = 4
            for s in shape[1:]:
                size *= s
            size = (size + 31) // 32 * 32
            if at is None:
                at = cursor[0]
                cursor[0] += size
            else:
                at, at_list = at[0], at
                at_list[0] += size
            assert at + size <= 229344, (name, at + size)
            return nc.alloc_sbuf_tensor_at(name, shape, dt, offset=at)

        def sem(name):
            return ctx.enter_context(nc.semaphore(name))

        ident = sb("ident", [P, P])
        ones = sb("ones", [P, P])
        three_halves = sb("three_halves", [P, 1])
        group_ones = sb("group_ones", [P, P])
        upto = sb("upto", [P, P])
        level_mask = sb("level_mask", [P, LEVELS, P])
        gain = sb("gain", [P, D])
        wab_hi = sb("wab_hi", [P, KT * 8 + P], f32r)
        wab_lo = sb("wab_lo", [P, KT * 8 + P], f32r)
        cw = sb("cw", [P, NH, 3, 4])
        scw = sb("scw", [P, 4, 3])
        scg = sb("scg", [P, 4, 1])
        gdng = sb("gdng", [P, 1])
        nega = sb("nega", [P, NH])
        dtb = sb("dtb", [P, NH])
        halo = sb("halo", [P, NH, 3, 3])
        sc_halo = sb("sc_halo", [P, 4, 2])
        state = sb("state", [P, NH, HD])
        kmem = sb("kmem", [P, KT, N_MEM])
        gate_ab = sb("gate_ab", [P, TT, 8])
        G = {k: sb("gate_" + k, [P, TT, NH]) for k in
             ("t0", "t1", "t2", "t3", "t4", "g", "gc", "beta", "nbeg", "fdec", "elast", "egc")}
        stat = {k: sb("stat_" + k, [P, 2]) for k in ("ss", "t", "l", "y", "u", "w", "v", "r")}
        act_hi_at = cursor[0]
        act_hi = sb("act_hi", [P, KT, HALF], f32r)
        act_lo_at = cursor[0]
        act_lo = sb("act_lo", [P, KT, HALF], f32r)
        w_hi = [sb(f"w_hi{i}", [P, D], f32r) for i in range(RING - 1)]
        slot3 = cursor[0]
        w_hi += [sb("w_hi3", [P, D], f32r)]
        w_lo = [sb(f"w_lo{i}", [P, D], f32r) for i in range(RING)]
        raw = [sb(f"raw{i}", [P, D]) for i in range(3)]
        overlay = cursor[0]
        row_hi = sb("row_hi", [P, 2, HALF], f32r)
        row_lo = sb("row_lo", [P, 2, HALF], f32r)
        w_hi += [sb(f"w_hi{i}", [P, D], f32r) for i in (4, 5)]
        w_lo += [sb(f"w_lo{i}", [P, D], f32r) for i in (4, 5)]
        h = sb("h", [P, TT, D])
        temps = cursor[0]
        xn = sb("xn", [P, 2, D])
        z = [overlay + 32768]
        conv_in = [sb(f"conv_in{i}", [P, 3 + HALF], at=z) for i in range(2)]
        conv_acc = sb("conv_acc", [P, 2, CH], at=z)
        stage = sb("stage", [P, 2, CH], at=z)
        ab_t = sb("ab_t", [P, HALF], at=[overlay])
        mem_in = sb("mem_in", [P, 2, D], at=[overlay + 8192])
        junk = sb("junk", [P, D], at=[overlay + 16384])
        junk_last = sb("junk_last", [P, D], at=[act_lo_at])
        result = sb("result", [P, TT, D], at=[act_hi_at])
        mix_first = sb("mix_first", [P, 2, D], at=[act_lo_at])
        gain_mix = sb("gain_mix", [P, D], at=[overlay + 20480])
        vmem = sb("vmem", [P, 2, D], at=[overlay])
        z = [overlay]
        sc_u = sb("sc_u", [P, 2 + HALF], at=z)
        sc_acc = sb("sc_acc", [P, 2, CH], at=z)
        sc_y = sb("sc_y", [P, 2, CH], at=z)
        qk = sb("qk", [P, 2, 2, NH, P], at=z)
        vv = sb("vv", [P, 2, NH, P], at=z)
        kqn = sb("kqn", [P, NH, 2, P], at=z)
        ge = sb("ge", [P, 2, NH, P], at=z)
        diff = sb("diff", [P, NH, P], at=z)
        dec = [sb("dec0", [P, 2, NH, P], at=z), sb("dec1", [P, 2, NH, P], at=[slot3])]
        am = sb("am", [P, 2, NH, P], at=z)
        kbg = sb("kbg", [P, NH, P], at=z)
        kdec = sb("kdec", [P, NH, P], at=z)
        vb = sb("vb", [P, NH, P], at=z)
        Xm = sb("Xm", [P, NH, P], at=z)
        Tm = sb("Tm", [P, NH, P], at=z)
        Ym = sb("Ym", [P, NH, P // 2], at=z)
        wt = sb("wt", [P, NH, P], at=z)
        vnew = sb("vnew", [P, NH, P], at=z)
        osq = sb("osq", [P, NH, P], at=z)
        on = osq
        oo = sb("oo", [P, NH, P], at=z)
        zz = sb("zz", [P, 2, NH, P], at=z)
        rn = sb("rn", [P, 2, NH, P], at=z)
        ost = {k: sb("ost_" + k, [P, NH], at=z) for k in ("ss", "t", "l", "y", "u", "v", "w", "r")}
        mixraw = xn
        z = [overlay + 16384]
        qT = sb("qT", [P, 2, HALF], at=z)
        pp = sb("pp", [P, 4, N_MEM], at=z)
        pT = sb("pT", [P, 2, CH], at=z)
        z = [cursor[0]]
        vh = sb("vh", [P, 2, XD], at=z)
        smx = sb("smx", [P, 3, 4], at=z)
        rsum = sb("rsum", [P, 4], at=z)
        z = [temps]
        sg = sb("sg", [P, 2, CH], at=z)
        aa = sb("aa", [P, 2, CH], at=z)
        PS = ctx.enter_context(nc.psum_tensor("PS", [P, 8, 512], f32))

        qkvz_d = nc.dram_tensor("qkvz_d", [4, NH, P, SEQ], f32, kind="Internal").ap()
        vmem_d = nc.dram_tensor("vmem_d", [P, 2, D], f32, kind="Internal").ap()
        mix_d = nc.dram_tensor("mix_d", [KT, P, SEQ], f32, kind="Internal").ap()

        S = {}

        def sems(names):
            for n in names.split():
                S[n] = sem(n)

        sems("const_in const_made nega_ready wab_raw wab_hi_ready wab_lo_ready gain_in")
        sems("raw_ready0 raw_ready1 raw_ready2 w_hi_ready w_lo_ready")
        sems("ss_ready ln_ready y_ready nstat xn_ready tr_full0 tr_full1 tr_hi tr_lo0 tr_lo1 "
             "out_stored")
        sems("km_full0 km_full1 km_out0 km_out1 vm_full vm_out vm_stored")
        sems("ab_full0 ab_full1 ab_out abt_full gate_step_dve gate_step_act gate_gc_full")
        for b in range(4):
            sems(f"qkvz_full{b} qkvz_out{b}")
        sems("halo_in conv_step conv_ready halo_out stage_ready st_stored0 st_stored1")
        sems("ld0 ld1 ldz0 ldz1 sq_ready rln_ready rn_ready gu_ready diff_ready egb_ready relu_ready "
             "dec_ready decm_ready am0_ready am_ready t1_ready kqn_ready qdec_ready kbg_ready "
             "kdec_ready vb_ready a_ready attn_ready x_ready t_ready ym_ready wt_ready vnew_ready "
             "s_ready osq_ready ossum_ready ost_ready oln_ready oy_ready ostep on_ready oo_ready "
             "o_stored")
        sems("gc_full nrm_full kt_full vt_full gram_full a1t_full y_full xy_full xt_full w_full "
             "vn_full o_full kv_full ont_full")
        sems("sc_full0 sc_full1 scn_full c_out u_ready sc_halo_in sc_halo_out sc_step0 sc_step1 "
             "scy_ready0 scy_ready1 scsq_ready scln_ready scr_ready scyn_ready y_stored")
        sems("row_full0 row_full1 row_out0 row_out1 h_in0 h_in1 h_in2 h_in3 mix_in0 mix_in1 "
             "mix_hi_ready mix_lo_ready")
        sems("q_full q_out s_full mx_ready p_exp rs_ready p_ready pt_full pt_out vh_ready "
             "pv_full ot_hi ot_lo mx_step")
        sems("gu_full0 gu_full1 sg_ready ga_ready0 ga_ready1 ah_ready al_ready0 al_ready1")

        def bank(b, n=1):
            return PS[:, b:b + n, :] if n > 1 else PS[:, b, :]

        def flat(ap):
            return ap.rearrange("p a b -> p (a b)")

        def over_tokens(ap):
            return ap.unsqueeze(2).broadcast_to([P, NH, P])

        def over_heads(ap):
            return ap.unsqueeze(1).broadcast_to([P, NH, P])

        def r4(ap):
            return ap.rearrange("p (h t) -> p h t", h=NH)

        def odd_blocks(t, l):
            return t.rearrange("p h (m e c) -> p (h m) e c", e=2, c=1 << l)[:, :, 1, :]

        U_QKVZ = 0
        U_MIX = U_QKVZ + QKVZ_UNITS
        U_OUT = U_MIX + MIX_UNITS
        U_ATT = U_OUT + OUT_UNITS
        U_FFN = U_ATT + ATT_UNITS

        def unit(half, k):
            return MEM_UNITS + half * HALF_UNITS + k

        L_QKVZ = 0
        L_MIX = L_QKVZ + QKVZ_UNITS // 2
        L_OUT = L_MIX + MIX_UNITS // 3
        L_ATT = L_OUT + OUT_UNITS // 2
        L_FFN = L_ATT + ATT_UNITS // 2
        HALF_LOADS = L_FFN + FFN_UNITS // 2

        def nth_load(half, before):
            return MEM_UNITS // 2 + half * HALF_LOADS + before + 1

        R_OUT, R_ATT, R_FFN = 0, KT // 2, KT // 2 + XH

        def norm_no(half, which, t):
            return 2 + (half * 4 + which) * TT + t

        def transposed(half, which):
            return 1 + (half * 3 + which) * (TT // 2)

        def gate(name, m):
            return over_tokens(G[name][:, bass.ds(m, 1), :].rearrange("p n h -> p (n h)"))

        def newton(pool, no, par):
            col = {k: v[:, par:par + 1] for k, v in stat.items()}
            own = S["nstat"]
            if not isinstance(no, int) or no >= 2:
                pool.wait_ge(S["xn_ready"], no - 1)
            pool.wait_ge(S["y_ready"], no + 1)
            pool.tensor_tensor(col["u"], col["y"], col["y"], ALU.mult).then_inc(own, 1)
            pool.wait_ge(own, no * 4 + 1)
            pool.tensor_tensor(col["w"], col["u"], col["t"], ALU.mult).then_inc(own, 1)
            pool.wait_ge(own, no * 4 + 2)
            pool.tensor_tensor(col["v"], three_halves[:, :], col["w"], ALU.subtract)\
                .then_inc(own, 1)
            pool.wait_ge(own, no * 4 + 3)
            pool.tensor_tensor(col["r"], col["v"], col["y"], ALU.mult).then_inc(own, 1)

        def newtons(pool, half, which):
            for t in range(TT):
                newton(pool, norm_no(half, which, t), t % 2)

        def decays_pool(pool, n, m, par):
            pool.wait_ge(S["dec_ready"], n + 1)
            pool.tensor_tensor(dec[par][:, 0, :, :], dec[par][:, 0, :, :], gate("beta", m),
                               ALU.mult).then_inc(S["decm_ready"], 1)
            pool.tensor_tensor(dec[par][:, 1, :, :], dec[par][:, 1, :, :], over_heads(upto[:, :]),
                               ALU.mult).then_inc(S["decm_ready"], 1)

        def chunk_pool(pool, half, m, par, j, last, split_lo):
            n = half * TT + m
            n_u = unit(half, U_MIX + j * 3)

            def blocks(l):
                if l == 1:
                    pool.wait_ge(S["a_ready"], n + 1)
                    pool.wait_ge(S["y_full"], n * 6)
                elif l == 2:
                    pool.wait_ge(S["a1t_full"], n + 1)
                    pool.wait_ge(S["t1_ready"], n + 1)
                else:
                    pool.wait_ge(S["y_full"], n * 6 + l - 2)
                pool.tensor_tensor(am[:, l % 2, :, :], dec[par][:, 0, :, :],
                                   over_heads(level_mask[:, l, :]), ALU.mult)\
                    .then_inc(S["am_ready"], 1)

            for step in STEPS:
                if step == "gram":
                    blocks(1)
                    blocks(2)
                if step in ("y1", "y2", "y3", "y4"):
                    blocks(int(step[1]) + 2)
                if step == "y3":
                    split_lo((n_u + 2, 2, 2) if par == 0 else (n_u + 4, 1, 1))
                if step == "y6" and par == 0:
                    split_lo((n_u + 3, 0, 0))
                if step == "x6" and not last:
                    decays_pool(pool, n + 1, m + 1, 1 - par)

        def ffn_pool(pool, half, j, split_lo, last):
            n_u = unit(half, U_FFN + j * 6)
            R = half * NPAIR + j
            for f in range(2):
                split_lo((n_u + 2 + 2 * f, 2 + 2 * f, 0))
                split_lo((n_u + 3 + 2 * f, 3 + 2 * f, 1))
                for c in range(2):
                    pool.wait_ge(S["ah_ready"], R * 4 + f * 2 + c + 1)
                    pool.tensor_tensor(row_lo[:, f, c * CH:(c + 1) * CH], aa[:, c, :],
                                       row_hi[:, f, c * CH:(c + 1) * CH].bitcast(f32),
                                       ALU.subtract).then_inc(S[f"al_ready{c}"], 1)
            if not last:
                split_lo((n_u + 6, 0, 0))
                split_lo((n_u + 7, 1, 1))

        def gates_act(act, half):
            dve, own = S["gate_step_dve"], S["gate_step_act"]
            k = half * GATE_ACT
            d = half * GATE_DVE
            act.wait_ge(dve, d + GD["min"])
            act.activation(G["t1"][:, :, :], G["t1"][:, :, :], ACT.Exp).then_inc(own, 1)
            act.wait_ge(dve, d + GD["bmin"])
            act.activation(G["beta"][:, :, :], G["beta"][:, :, :], ACT.Exp).then_inc(own, 1)
            act.wait_ge(dve, d + GD["w1"])
            act.activation(G["t3"][:, :, :], G["t2"][:, :, :], ACT.Ln).then_inc(own, 1)

        def gates_act_late(act, half):
            dve, own = S["gate_step_dve"], S["gate_step_act"]
            d = half * GATE_DVE
            act.wait_ge(dve, d + GD["fd"])
            act.activation(G["egc"][:, :, :], G["gc"][:, :, :], ACT.Exp).then_inc(own, 1)
            act.activation(G["elast"][:, :, :], G["t0"][:, :, :], ACT.Exp).then_inc(own, 1)
            act.activation(G["fdec"][:, :, :], G["t1"][:, :, :], ACT.Exp).then_inc(own, 1)

        def silu_store(act, half, j, R, g):
            u, c = g // 2, g % 2
            act.wait_ge(S["conv_ready"], R * 6 + g + 1)
            act.wait_ge(S[f"st_stored{c}"], (R * 4 + g // 2) * 16)
            act.activation(stage[:, c, :], conv_acc[:, c, :], ACT.Silu)\
                .then_inc(S["stage_ready"], 1)
            act.wait_ge(S["stage_ready"], R * 8 + g + 1)
            store_stage(act, half, j, u, c)

        def store_stage(act, half, j, u, c):
            act.dma_start(qkvz_d[u, bass.ds(j, 1), :, bass.ds(half * HALF + c * CH, CH)]
                          .rearrange("n p c -> p (n c)"), stage[:, c, :])\
                .then_inc(S[f"st_stored{c}"], 16)

        def silu_z(act, half, j, R, g):
            c, b = g % 2, g % 4
            act.wait_ge(S[f"qkvz_full{b}"], R * 2 + g // 4 + 1)
            act.wait_ge(S[f"st_stored{c}"], (R * 4 + 3) * 16)
            act.activation(stage[:, c, :], bank(b), ACT.Silu).then_inc(S["stage_ready"], 1)
            act.wait_ge(S["stage_ready"], R * 8 + g + 1)
            store_stage(act, half, j, 3, c)

        def load_chunk(act, half, m, par):
            cols = bass.ds(half * HALF + m * P, P)
            for i in range(2):
                act.dma_start(qk[:, par, i, :, :],
                              qkvz_d[i, :, :, cols].rearrange("h p t -> p h t"))\
                    .then_inc(S[f"ld{par}"], 16)
            act.dma_start(vv[:, par, :, :], qkvz_d[2, :, :, cols].rearrange("h p t -> p h t"))\
                .then_inc(S[f"ld{par}"], 16)

        def load_z(act, half, m, par):
            act.dma_start(zz[:, par, :, :], qkvz_d[3, :, :, bass.ds(half * HALF + m * P, P)]
                          .rearrange("h p t -> p h t")).then_inc(S[f"ldz{par}"], 16)

        def load_mix(act, half, kk):
            act.dma_start((mix_first if kk < 2 else mixraw)[:, kk % 2, :],
                          mix_d[(kk + KT // 2) % KT, :, bass.ds(half * HALF, HALF)])\
                .then_inc(S[f"mix_in{kk % 2}"], 16)

        def hflat(t):
            return t.rearrange("p h t -> p (h t)")

        def pair(t):
            return t.rearrange("p a h t -> p a (h t)")

        def squares(act, half, m, par):
            n = half * TT + m
            act.wait_ge(S[f"ld{par}"], (n - par) * 24 + 48)
            act.wait_ge(S["kqn_ready"], n * 2)
            act.activation(pair(rn[:, :, :, :]), pair(qk[:, par, :, :, :]), ACT.Square)\
                .then_inc(S["sq_ready"], 1)

        def exp_gc(act, n, par):
            act.wait_ge(S["gc_full"], n + 1)
            act.wait_ge(S["diff_ready"], n + 1)
            act.activation(hflat(ge[:, par, :, :]), bank(7), ACT.Exp).then_inc(S["egb_ready"], 1)

        def relus(act, n, par, finished):
            act.wait_ge(S["diff_ready"], n + 1)
            act.wait_ge(S["am_ready"], finished * 6)
            act.wait_ge(S["o_full"], finished)
            for i, sign in enumerate((1.0, -1.0)):
                act.activation(hflat(dec[par][:, i, :, :]), hflat(diff[:, :, :]), ACT.Relu,
                               scale=sign).then_inc(S["relu_ready"], 1)

        def exp_decays(act, n, par):
            act.wait_ge(S["relu_ready"], n * 2 + 2)
            act.activation(pair(dec[par][:, :, :, :]), pair(dec[par][:, :, :, :]), ACT.Exp,
                           scale=-1.0).then_inc(S["dec_ready"], 1)

        def ln_norms(act, n):
            act.wait_ge(S["nrm_full"], n + 1)
            act.activation(pair(rn[:, :, :, :]), bank(6, 2), ACT.Ln, bias=EPS)\
                .then_inc(S["rln_ready"], 1)

        def exp_norms(act, n):
            act.wait_ge(S["rln_ready"], n + 1)
            act.activation(pair(rn[:, :, :, :]), pair(rn[:, :, :, :]), ACT.Exp, scale=-0.5)\
                .then_inc(S["rn_ready"], 1)

        def rms_estimate(act, n):
            act.wait_ge(S["ost_ready"], n + 1)
            act.activation(ost["l"][:, :], ost["t"][:, :], ACT.Ln).then_inc(S["oln_ready"], 1)
            act.wait_ge(S["oln_ready"], n + 1)
            act.activation(ost["y"][:, :], ost["l"][:, :], ACT.Exp, scale=-0.5)\
                .then_inc(S["oy_ready"], 1)

        def store_o(act, half, m):
            act.wait_ge(S["oo_ready"], half * TT + m + 1)
            act.dma_start(mix_d[0:NH, :, bass.ds(half * HALF + m * P, P)]
                          .rearrange("h p t -> p h t"), oo[:, :, :]).then_inc(S["o_stored"], 16)

        def sc_squares(act, R, c):
            act.wait_ge(S[f"scy_ready{c}"], R + 1)
            act.activation(sc_acc[:, c, :], sc_y[:, c, :], ACT.Square).then_inc(S["scsq_ready"], 1)

        def sc_rms(act, R, c):
            act.wait_ge(S["scn_full"], R * 2 + c + 1)
            act.activation(sc_acc[:, c, :], bank(2), ACT.Ln, bias=EPS, scale=1.0 / 64)\
                .then_inc(S["scln_ready"], 1)
            act.wait_ge(S["scln_ready"], R * 2 + c + 1)
            act.activation(sc_acc[:, c, :], sc_acc[:, c, :], ACT.Exp, scale=-0.5)\
                .then_inc(S["scr_ready"], 1)

        def store_sc(act, half, j, c):
            act.wait_ge(S["scyn_ready"], (half * 4 + j) * 2 + c + 1)
            act.dma_start(mix_d[bass.ds(j + 4, 1), :, bass.ds(half * HALF + c * CH, CH)]
                          .rearrange("n p t -> p (n t)"), sc_y[:, c, :])\
                .then_inc(S["y_stored"], 16)

        def start_act(act, half):
            n = half * TT
            load_chunk(act, half, 0, 0)
            load_z(act, half, 0, 0)
            squares(act, half, 0, 0)
            exp_gc(act, n, 0)
            relus(act, n, 0, n)
            ln_norms(act, n)
            exp_norms(act, n)
            exp_decays(act, n, 0)

        def chunk_act(act, half, m, par, j, first, last, split_hi):
            n = half * TT + m
            R = half * 4 + j
            for step in STEPS:
                l = int(step[1]) if step[0] in "yx" else 0
                if step == "gram":
                    if not first:
                        if par == 0:
                            sc_rms(act, R - 1, 0)
                        rms_estimate(act, n - 1)
                    if not last:
                        act.wait_ge(S["vt_full"], n)
                        load_chunk(act, half, m + 1, 1 - par)
                if step[0] == "y":
                    if l > 1:
                        act.wait_ge(S["xt_full"], n * 5 + l - 1)
                        act.wait_ge(S["xy_full"], n * 6 + l - 1)
                        act.activation(hflat(Tm[:, :, :]), bank(5), ACT.Copy)\
                            .then_inc(S["t_ready"], 1)
                    act.wait_ge(S["y_full"], n * 6 + l)
                    act.wait_ge(S["xy_full"], n * 6 + l - 1)
                    act.activation(hflat(Ym[:, :, :]), bank(3)[:, 0:NH * P // 2], ACT.Copy)\
                        .then_inc(S["ym_ready"], 1)
                if par == 0 and step == "y2":
                    act.wait_ge(S["sc_full0"], R * 3 + 1)
                    act.wait_ge(S["sc_halo_out"], R)
                    act.activation(sc_u[:, 2:2 + CH], bank(0), ACT.Copy).then_inc(S["c_out"], 1)
                if par == 0 and step == "y6":
                    act.wait_ge(S["sc_full1"], R * 3 + 1)
                    act.activation(sc_u[:, 2 + CH:2 + 2 * CH], bank(1), ACT.Copy)\
                        .then_inc(S["c_out"], 1)
                if step == "y3":
                    act.wait_ge(S["sc_full1"], R * 3 + 2 * par)
                    if par == 0:
                        split_hi(R + 1, 2, 2)
                    else:
                        split_hi(nth_load(half, L_MIX + j + 1), 1, 1)
                if par == 0 and step == "y6":
                    split_hi(nth_load(half, L_MIX + j + 1), 0, 0)
                if par == 0 and not first:
                    if step == "y2":
                        store_sc(act, half, j - 1, 0)
                        sc_squares(act, R - 1, 1)
                    if step == "y4":
                        sc_rms(act, R - 1, 1)
                    if step == "y5":
                        store_sc(act, half, j - 1, 1)
                if step == "x3" and not last:
                    squares(act, half, m + 1, 1 - par)
                if step == "y4":
                    if not first:
                        store_o(act, half, m - 1)
                    if not last:
                        load_z(act, half, m + 1, 1 - par)
                if step == "y5" and not last:
                    exp_gc(act, n + 1, 1 - par)
                if step == "x5" and not last:
                    relus(act, n + 1, 1 - par, n)
                if step == "y6" and not last:
                    ln_norms(act, n + 1)
                if step == "x6" and not last:
                    exp_norms(act, n + 1)
                if step == "w":
                    act.wait_ge(S["w_full"], n + 1)
                    act.wait_ge(S["vn_full"], n)
                    act.activation(hflat(wt[:, :, :]), bank(7), ACT.Copy).then_inc(S["wt_ready"], 1)
                    if not last:
                        exp_decays(act, n + 1, 1 - par)
                if step == "v":
                    act.wait_ge(S["vn_full"], n + 1)
                    act.wait_ge(S["kv_full"], n)
                    act.activation(hflat(vnew[:, :, :]), bank(3), ACT.Copy)\
                        .then_inc(S["vnew_ready"], 1)
                    if par == 1:
                        sc_squares(act, R, 0)
                if step == "o":
                    act.wait_ge(S["o_full"], n + 1)
                    act.wait_ge(S["ont_full"], n)
                    act.activation(hflat(osq[:, :, :]), bank(4), ACT.Square)\
                        .then_inc(S["osq_ready"], 1)

        def end_act(act, half):
            R = half * 4 + 3
            act.wait_ge(S["sc_full1"], (R + 1) * 3)
            act.wait_ge(S["scy_ready0"], R + 1)
            for k in range(2):
                load_mix(act, half, k)
            sc_rms(act, R, 0)
            sc_squares(act, R, 1)
            rms_estimate(act, half * TT + TT - 1)
            sc_rms(act, R, 1)
            store_sc(act, half, 3, 0)
            store_sc(act, half, 3, 1)
            store_o(act, half, TT - 1)

        def att_q_out(act, R, g, scored):
            c, dt = g // 2, g % 2
            act.wait_ge(S["q_full"], R * 4 + g + 1)
            act.wait_ge(S["s_full"], scored)
            act.activation(qT[:, dt, c * CH:(c + 1) * CH], bank((4 if c else 2) + dt), ACT.Copy)\
                .then_inc(S["q_out"], 1)

        def att_act(act, half, j, split_hi, last):
            R = half * XH + j
            act.wait_ge(S["row_full1"], (half * ROW_PASSES + R_ATT + j) * 4)
            for u in range(2):
                split_hi(nth_load(half, L_ATT + j * 2 + 1), 2 + u, u)

            def q_out(g):
                att_q_out(act, R, g, R * 2)

            def softmax(c):
                act.wait_ge(S["mx_ready"], R * 2 + c + 1)
                act.wait_ge(S["pt_full"], R * 2 + c)
                act.wait_ge(S["rs_ready"], R * 2 + c)
                for t in range(4):
                    act.activation(pp[:, t, :], PS[:, 6 + t // 2, (t % 2) * N_MEM:(t % 2 + 1) * N_MEM],
                                   ACT.Exp, bias=smx[:, 0, t:t + 1], scale=XD ** -0.5,
                                   accum_out=smx[:, 1, t:t + 1]).then_inc(S["p_exp"], 1)

            def pt_out(c):
                act.wait_ge(S["pt_full"], R * 2 + c + 1)
                act.wait_ge(S["pv_full"], R * 2 + c)
                act.activation(flat(pT[:, :, :]), flat(bank(4, 2)), ACT.Copy)\
                    .then_inc(S["pt_out"], 1)

            def o_hi(c):
                act.wait_ge(S["pv_full"], R * 2 + c + 1)
                act.wait_ge(S["row_full1"], (half * ROW_PASSES + R_ATT + j) * 4)
                act.activation(row_hi[:, :, c * CH:(c + 1) * CH], bank(6 * c, 2), ACT.Copy)\
                    .then_inc(S["ot_hi"], 1)

            q_out(2)
            softmax(0)
            q_out(3)
            for u in range(2):
                split_hi(nth_load(half, L_ATT + j * 2 + 2), u, u)
            pt_out(0)
            softmax(1)
            o_hi(0)
            if not last:
                att_q_out(act, R + 1, 0, R * 2 + 1)
            pt_out(1)
            if not last:
                att_q_out(act, R + 1, 1, R * 2 + 1)
            o_hi(1)

        def ffn_act(act, half, j, split_hi, last):
            R = half * NPAIR + j
            for f in range(2):
                if f == 1:
                    act.wait_ge(S["row_full1"], (half * ROW_PASSES + R_FFN + j) * 4)
                for u in range(2):
                    split_hi(nth_load(half, L_FFN + j * 3 + 1 + f), 2 + 2 * f + u, u)
                for c in range(2):
                    act.wait_ge(S[f"gu_full{c}"], R * 2 + f + 1)
                    act.wait_ge(S[f"ga_ready{c}"], R * 2 + f)
                    act.activation(sg[:, c, :], bank(4 + 2 * c), ACT.Silu)\
                        .then_inc(S["sg_ready"], 1)
                    act.wait_ge(S[f"ga_ready{c}"], R * 2 + f + 1)
                    act.wait_ge(S["row_full1"], (half * ROW_PASSES + R_FFN + j) * 4)
                    act.activation(row_hi[:, f, c * CH:(c + 1) * CH], aa[:, c, :], ACT.Copy)\
                        .then_inc(S["ah_ready"], 1)
            if not last:
                for u in range(2):
                    split_hi(nth_load(half, L_FFN + j * 3 + 3), u, u)

        def gates_dve(dve, half, late):
            own, sact = S["gate_step_dve"], S["gate_step_act"]
            d = half * GATE_DVE
            k = half * GATE_ACT
            count = [GD["b2"] if late else 0]

            def step(name, op, wait_act=0):
                if count[0]:
                    dve.wait_ge(own, d + count[0])
                if wait_act:
                    dve.wait_ge(sact, k + wait_act)
                op().then_inc(own, 1)
                count[0] += 1
                assert GD.get(name, count[0]) == count[0], (name, count[0])

            g = {k: v[:, :, :] for k, v in G.items()}
            if late:
                dve.wait_ge(S["gate_gc_full"], half + 1)
                step("gc", lambda: dve.tensor_copy(flat(g["gc"]), PS[:, 7, 0:TT * NH]))
                step("gl", lambda: dve.tensor_copy(flat(g["t0"]), PS[:, 7, TT * NH:2 * TT * NH]))
                step("fd", lambda: dve.tensor_tensor(g["t1"], g["t0"], g["gc"], ALU.subtract))
                step("nb", lambda: dve.tensor_tensor(g["nbeg"], g["beta"], g["egc"], ALU.mult), 6)
                step("nn", lambda: dve.tensor_scalar(g["nbeg"], g["nbeg"], -1.0, None, ALU.mult))
                assert count[0] == GATE_DVE
                return
            a_in, b_in = gate_ab[:, :, 0:NH], gate_ab[:, :, NH:2 * NH]
            dve.wait_ge(S["abt_full"], half + 1)
            dve.wait_ge(S["oo_ready"], half * TT)
            step("copy", lambda: dve.tensor_copy(
                gate_ab[:, :, :],
                bank(6, 2).rearrange("p b (t c) -> p (b t) c", t=4)[:, :, 0:2 * NH]))
            tile_bias = dtb[:, :].unsqueeze(1).broadcast_to([P, TT, NH])
            tile_nega = nega[:, :].unsqueeze(1).broadcast_to([P, TT, NH])
            step("a", lambda: dve.tensor_tensor(g["t0"], a_in, tile_bias, ALU.add))
            step("neg", lambda: dve.tensor_scalar(g["t1"], g["t0"], -1.0, None, ALU.mult))
            step("min", lambda: dve.tensor_tensor(g["t1"], g["t1"], g["t0"], ALU.min))
            step("bmin", lambda: dve.tensor_scalar(g["beta"], b_in, -1.0, 80.0, ALU.mult, ALU.min))
            step("w1", lambda: dve.tensor_scalar(g["t2"], g["t1"], 1.0, None, ALU.add), 1)
            step("wm", lambda: dve.tensor_scalar(g["t4"], g["t2"], -1.0, None, ALU.add))
            step("eq", lambda: dve.tensor_scalar(g["g"], g["t4"], 0.0, None, ALU.is_equal))
            step("mx", lambda: dve.tensor_scalar(g["t4"], g["t4"], 1e-30, None, ALU.max))
            step("rc", lambda: dve.reciprocal(g["t4"], g["t4"]))
            step("l1", lambda: dve.tensor_tensor(g["t3"], g["t3"], g["t4"], ALU.mult), 3)
            step("l2", lambda: dve.tensor_tensor(g["t3"], g["t3"], g["g"], ALU.add))
            step("l3", lambda: dve.tensor_tensor(g["t3"], g["t3"], g["t1"], ALU.mult))
            step("sp", lambda: dve.scalar_tensor_tensor(flat(g["t3"]), flat(g["t0"]), 0.0,
                                                        flat(g["t3"]), ALU.max, ALU.add))
            step("g", lambda: dve.tensor_tensor(g["g"], g["t3"], tile_nega, ALU.mult))
            step("b1", lambda: dve.tensor_scalar(g["beta"], g["beta"], 1.0, None, ALU.add), 2)
            step("b2", lambda: dve.reciprocal(g["beta"], g["beta"]))

        def conv_dve(dve, R, j, u, c, g, ci):
            b = g % 4
            dve.wait_ge(S[f"qkvz_out{b}"], CONV_OUT[g] + R * CONV_OUT_PER[b])
            dve.wait_ge(S["halo_in"], R * 3 + u + 1)
            dve.wait_ge(S["stage_ready"], R * 8 + g - 1 if g >= 2 else R * 8)
            acc = conv_acc[:, c, :]
            k = (R * 6 + g) * 3

            def tap(i):
                return cw[:, bass.ds(j, 1), u, i:i + 1].rearrange("p n k -> p (n k)")

            dve.tensor_scalar(acc, ci[:, c * CH:c * CH + CH], tap(0), None, ALU.mult)\
                .then_inc(S["conv_step"], 1)
            for i in (1, 2):
                dve.wait_ge(S["conv_step"], k + i)
                dve.scalar_tensor_tensor(acc, ci[:, c * CH + i:c * CH + i + CH], tap(i), acc,
                                         ALU.mult, ALU.add).then_inc(S["conv_step"], 1)
            dve.wait_ge(S["conv_step"], k + 3)
            dve.scalar_tensor_tensor(acc, ci[:, c * CH + 3:c * CH + 3 + CH], tap(3), acc,
                                     ALU.mult, ALU.add).then_inc(S["conv_ready"], 1)

        def triangle_g(dve, m, par, finished):
            dve.wait_ge(S["o_full"], finished)
            dve.tensor_tensor(ge[:, par, :, :], over_heads(upto[:, :]), gate("g", m), ALU.mult)\
                .then_inc(S["gu_ready"], 1)

        def differences(dve, n, m):
            dve.wait_ge(S["gc_full"], n + 1)
            dve.wait_ge(S["relu_ready"], n * 2)
            dve.tensor_tensor(diff[:, :, :], r4(bank(7)), gate("gc", m), ALU.subtract)\
                .then_inc(S["diff_ready"], 1)

        def normalise(dve, n, par):
            dve.wait_ge(S["rn_ready"], n + 1)
            dve.wait_ge(S["gram_full"], n)
            dve.tensor_tensor(kqn[:, :, 0, :], qk[:, par, 1, :, :], rn[:, 1, :, :], ALU.mult)\
                .then_inc(S["kqn_ready"], 1)
            dve.scalar_tensor_tensor(kqn[:, :, 1, :], qk[:, par, 0, :, :], HD ** -0.5,
                                     rn[:, 0, :, :], ALU.mult, ALU.mult)\
                .then_inc(S["kqn_ready"], 1)
            dve.wait_ge(S["egb_ready"], n + 1)
            dve.wait_ge(S["kqn_ready"], n * 2 + 2)
            dve.tensor_tensor(ge[:, par, :, :], ge[:, par, :, :], kqn[:, :, 1, :], ALU.mult)\
                .then_inc(S["qdec_ready"], 1)

        def normalise_o(dve, n):
            k = n * 4
            dve.wait_ge(S["oy_ready"], n + 1)
            dve.tensor_tensor(ost["u"][:, :], ost["y"][:, :], ost["y"][:, :], ALU.mult)\
                .then_inc(S["ostep"], 1)
            dve.wait_ge(S["ostep"], k + 1)
            dve.tensor_tensor(ost["v"][:, :], ost["u"][:, :], ost["t"][:, :], ALU.mult)\
                .then_inc(S["ostep"], 1)
            dve.wait_ge(S["ostep"], k + 2)
            dve.tensor_scalar(ost["w"][:, :], ost["v"][:, :], -0.5, 1.5, ALU.mult, ALU.add)\
                .then_inc(S["ostep"], 1)
            dve.wait_ge(S["ostep"], k + 3)
            dve.tensor_tensor(ost["r"][:, :], ost["w"][:, :], ost["y"][:, :], ALU.mult)\
                .then_inc(S["ostep"], 1)
            dve.wait_ge(S["ostep"], k + 4)
            dve.tensor_tensor(on[:, :, :], r4(bank(4)), over_tokens(ost["r"][:, :]), ALU.mult)\
                .then_inc(S["on_ready"], 1)

        def output_o(dve, n, m, par):
            dve.wait_ge(S["ont_full"], n + 1)
            dve.wait_ge(S["o_stored"], n * 16)
            dve.wait_ge(S[f"ldz{par}"], (n - par) * 8 + 16)
            dve.scalar_tensor_tensor(hflat(oo[:, :, :]), bank(7), gdng[:, 0:1],
                                     hflat(zz[:, par, :, :]), ALU.mult, ALU.mult)\
                .then_inc(S["oo_ready"], 1)

        def sc_tap(dve, R, j, c, i):
            w = scw[:, bass.ds(j, 1), i:i + 1].rearrange("p n k -> p (n k)")
            src = sc_u[:, c * CH + i:c * CH + i + CH]
            if i == 0:
                dve.wait_ge(S["u_ready"], R * 2 + c + 1)
                dve.wait_ge(S["sc_halo_in"], R + 1)
                dve.wait_ge(S["scyn_ready"], R * 2)
                dve.tensor_scalar(sc_acc[:, c, :], src, w, None, ALU.mult)\
                    .then_inc(S[f"sc_step{c}"], 1)
            else:
                dve.wait_ge(S[f"sc_step{c}"], R * 3 + i)
                dve.scalar_tensor_tensor(sc_acc[:, c, :], src, w, sc_acc[:, c, :], ALU.mult, ALU.add)\
                    .then_inc(S[f"sc_step{c}"], 1)

        def sc_u_product(dve, R, c):
            u = sc_u[:, 2 + c * CH:2 + (c + 1) * CH]
            dve.wait_ge(S[f"sc_full{c}"], R * 3 + 2)
            dve.wait_ge(S["c_out"], R * 2 + c + 1)
            dve.tensor_tensor(u, u, bank(c), ALU.mult).then_inc(S["u_ready"], 1)

        def sc_y_product(dve, R, c):
            dve.wait_ge(S[f"sc_step{c}"], R * 3 + 3)
            dve.wait_ge(S[f"sc_full{c}"], R * 3 + 3)
            dve.wait_ge(S["y_stored"], R * 32)
            dve.tensor_tensor(sc_y[:, c, :], sc_acc[:, c, :], bank(c), ALU.mult)\
                .then_inc(S[f"scy_ready{c}"], 1)

        def sc_normalise(dve, R, j, c):
            dve.wait_ge(S["scr_ready"], R * 2 + c + 1)
            dve.wait_ge(S[f"scy_ready{c}"], R + 1)
            dve.scalar_tensor_tensor(
                sc_y[:, c, :], sc_y[:, c, :], scg[:, bass.ds(j, 1), :].rearrange("p n k -> p (n k)"),
                sc_acc[:, c, :], ALU.mult, ALU.mult).then_inc(S["scyn_ready"], 1)

        def start_dve(dve, half):
            triangle_g(dve, 0, 0, half * TT)
            differences(dve, half * TT, 0)
            normalise(dve, half * TT, 0)

        def chunk_dve(dve, half, m, par, j, first, last):
            n = half * TT + m
            R = half * 4 + j
            A = dec[par]
            gram = bank(5, 2).rearrange("p b (h s t) -> p b h s t", h=2, s=2)
            two = lambda t: t.rearrange("p (b h) t -> p b h t", b=2)
            for step in STEPS:
                l = int(step[1]) if step[0] in "yx" else 0
                if step == "gram":
                    dve.wait_ge(S["gram_full"], n + 1)
                    dve.wait_ge(S["decm_ready"], n * 2 + 2)
                    dve.tensor_tensor(two(A[:, 0, :, :]), gram[:, :, :, 0, :], two(A[:, 0, :, :]),
                                      ALU.mult).then_inc(S["a_ready"], 1)
                    dve.wait_ge(S["a_ready"], n + 1)
                    dve.wait_ge(S["y_full"], n * 6)
                    dve.tensor_tensor(am[:, 0, :, :], A[:, 0, :, :], over_heads(level_mask[:, 0, :]),
                                      ALU.mult).then_inc(S["am0_ready"], 1)
                    dve.wait_ge(S["am0_ready"], n + 1)
                    dve.wait_ge(S["xy_full"], n * 6)
                    dve.tensor_tensor(Tm[:, :, :], over_heads(ident[:, :]), am[:, 0, :, :],
                                      ALU.subtract).then_inc(S["t1_ready"], 1)
                if step == "a1t":
                    dve.wait_ge(S["a1t_full"], n + 1)
                    dve.wait_ge(S["vn_full"], n)
                    dve.tensor_tensor(Xm[:, :, :], over_heads(ident[:, :]), r4(bank(2)),
                                      ALU.subtract).then_inc(S["x_ready"], 1)
                    dve.wait_ge(S["vt_full"], n + 1)
                    dve.tensor_tensor(vb[:, :, :], r4(bank(3)), gate("beta", m), ALU.mult)\
                        .then_inc(S["vb_ready"], 1)
                    if par == 1:
                        sc_u_product(dve, R, 0)
                    elif not first:
                        sc_y_product(dve, R - 1, 1)
                if step == "y1":
                    if not first:
                        normalise_o(dve, n - 1)
                    dve.tensor_tensor(two(A[:, 1, :, :]), gram[:, :, :, 1, :], two(A[:, 1, :, :]),
                                      ALU.mult).then_inc(S["attn_ready"], 1)
                if step[0] == "x":
                    dve.wait_ge(S["xy_full"], n * 6 + l)
                    dve.wait_ge(S["x_ready"], n * LEVELS + l)
                    dve.tensor_tensor(
                        odd_blocks(Xm[:, :, :], l), odd_blocks(Xm[:, :, :], l),
                        bank(4)[:, 0:NH * P // 2].rearrange("p (m c) -> p m c", c=1 << l),
                        ALU.subtract).then_inc(S["x_ready"], 1)
                if step == "x1":
                    dve.wait_ge(S["kt_full"], n + 1)
                    dve.wait_ge(S["w_full"], n)
                    dve.tensor_tensor(kbg[:, :, :], r4(bank(7)), gate("nbeg", m), ALU.mult)\
                        .then_inc(S["kbg_ready"], 1)
                    if par == 0 and not first:
                        sc_normalise(dve, R - 1, j - 1, 0)
                if step == "x2":
                    dve.wait_ge(S["kv_full"], n)
                    dve.tensor_tensor(kdec[:, :, :], r4(bank(7)), gate("fdec", m), ALU.mult)\
                        .then_inc(S["kdec_ready"], 1)
                    if par == 1:
                        sc_u_product(dve, R, 1)
                if step == "y3" and not last:
                    triangle_g(dve, m + 1, 1 - par, n)
                if step == "x3" and not first:
                    output_o(dve, n - 1, m - 1, 1 - par)
                if step == "x4":
                    if not last:
                        differences(dve, n + 1, m + 1)
                    if par == 0 and not first:
                        sc_normalise(dve, R - 1, j - 1, 1)
                if par == 1 and step in ("y3", "y4", "y5"):
                    for i, c in {"y3": ((0, 0), (1, 0)), "y4": ((2, 0), (0, 1)),
                                 "y5": ((1, 1), (2, 1))}[step]:
                        sc_tap(dve, R, j, c, i)
                if par == 1 and step == "y6":
                    dve.tensor_copy(sc_halo[:, bass.ds(j, 1), :].rearrange("p n k -> p (n k)"),
                                    sc_u[:, HALF:HALF + 2]).then_inc(S["sc_halo_out"], 1)
                if par == 0 and step == "y6":
                    dve.wait_ge(S["sc_halo_out"], R)
                    dve.tensor_copy(sc_u[:, 0:2], sc_halo[:, bass.ds(j, 1), :]
                                    .rearrange("p n k -> p (n k)")).then_inc(S["sc_halo_in"], 1)
                if step == "x6" and par == 1:
                    sc_y_product(dve, R, 0)
                if step == "w" and not last:
                    normalise(dve, n + 1, 1 - par)
                if step == "o":
                    dve.wait_ge(S["kv_full"], n + 1)
                    dve.wait_ge(S["s_ready"], n * 4)
                    for hh in range(NH):
                        dve.scalar_tensor_tensor(
                            state[:, hh, :], state[:, hh, :],
                            G["elast"][:, bass.ds(m, 1), hh:hh + 1].rearrange("p n h -> p (n h)"),
                            r4(bank(5))[:, hh, :], ALU.mult, ALU.add).then_inc(S["s_ready"], 1)
                    dve.wait_ge(S["osq_ready"], n + 1)
                    dve.tensor_reduce(ost["ss"][:, :], osq[:, :, :], AX.X, ALU.add)\
                        .then_inc(S["ossum_ready"], 1)
                    dve.wait_ge(S["ossum_ready"], n + 1)
                    dve.tensor_scalar(ost["t"][:, :], ost["ss"][:, :], 1.0 / HD, EPS, ALU.mult,
                                      ALU.add).then_inc(S["ost_ready"], 1)

        def end_dve(dve, half):
            R = half * 4 + 3
            n = half * TT + TT - 1
            sc_y_product(dve, R, 1)
            sc_normalise(dve, R, 3, 0)
            normalise_o(dve, n)
            sc_normalise(dve, R, 3, 1)
            output_o(dve, n, TT - 1, 1)

        def att_dve(dve, half, j):
            R = half * XH + j

            def row_max(c):
                dve.wait_ge(S["s_full"], R * 2 + c + 1)
                dve.wait_ge(S["p_exp"], (R * 2 + c) * 4)
                dve.tensor_reduce(smx[:, 2, :],
                                  bank(6, 2).rearrange("p b (t m) -> p (b t) m", t=2), AX.X, ALU.max)\
                    .then_inc(S["mx_step"], 1)
                dve.wait_ge(S["mx_step"], R * 2 + c + 1)
                dve.tensor_scalar(smx[:, 0, :], smx[:, 2, :], -XD ** -0.5, None, ALU.mult)\
                    .then_inc(S["mx_ready"], 1)

            def scale(c):
                dve.wait_ge(S["p_exp"], (R * 2 + c + 1) * 4)
                dve.wait_ge(S["p_ready"], R * 2 + c)
                dve.reciprocal(rsum[:, :], smx[:, 1, :]).then_inc(S["rs_ready"], 1)
                dve.wait_ge(S["rs_ready"], R * 2 + c + 1)
                dve.tensor_tensor(pp[:, :, :], pp[:, :, :],
                                  rsum[:, :].unsqueeze(2).broadcast_to([P, 4, N_MEM]), ALU.mult)\
                    .then_inc(S["p_ready"], 1)

            def o_lo(c):
                dve.wait_ge(S["ot_hi"], R * 2 + c + 1)
                dve.tensor_tensor(row_lo[:, :, c * CH:(c + 1) * CH], bank(6 * c, 2),
                                  row_hi[:, :, c * CH:(c + 1) * CH].bitcast(f32), ALU.subtract)\
                    .then_inc(S["ot_lo"], 1)

            row_max(0)
            scale(0)
            row_max(1)
            scale(1)
            o_lo(0)
            o_lo(1)

        def ffn_dve(dve, half, j):
            R = half * NPAIR + j
            for f in range(2):
                for c in range(2):
                    dve.wait_ge(S["sg_ready"], R * 4 + f * 2 + c + 1)
                    dve.wait_ge(S[f"al_ready{c}"], R * 2 + f)
                    dve.tensor_tensor(aa[:, c, :], sg[:, c, :], bank(5 + 2 * c), ALU.mult)\
                        .then_inc(S[f"ga_ready{c}"], 1)

        def sums_gc(pe, n, par):
            pe.wait_ge(S["gu_ready"], n + 1)
            nc.tensor.matmul(bank(7), ones[:, :], hflat(ge[:, par, :, :]), start=True, stop=True)\
                .then_inc(S["gc_full"], 1)

        def sums_norm(pe, n):
            pe.wait_ge(S["sq_ready"], n + 1)
            pe.wait_ge(S["diff_ready"], n + 1)
            pe.wait_ge(S["egb_ready"], n + 1)
            nc.tensor.matmul(bank(6), ones[:, :], hflat(rn[:, 0, :, :]), start=True, stop=True)
            nc.tensor.matmul(bank(7), ones[:, :], hflat(rn[:, 1, :, :]), start=True, stop=True)\
                .then_inc(S["nrm_full"], 1)

        def transpose_o(pe, n):
            pe.wait_ge(S["on_ready"], n + 1)
            for hh in range(NH):
                last = nc.tensor.transpose(r4(bank(7))[:, hh, :], on[:, hh, :], ident[:, :])
            last.then_inc(S["ont_full"], 1)

        def sc_sums(pe, R, c):
            pe.wait_ge(S["scsq_ready"], R * 2 + c + 1)
            pe.wait_ge(S["scln_ready"], R * 2 + c)
            nc.tensor.matmul(bank(2), group_ones[:, :], sc_acc[:, c, :], start=True, stop=True)\
                .then_inc(S["scn_full"], 1)

        def chunk_step_pe(pe, half, m, par, j, step, first, last):
            n = half * TT + m
            R = half * 4 + j
            l = int(step[1]) if step[0] in "yx" else 0
            if step == "start" and first:
                sums_gc(pe, n, 0)
                sums_norm(pe, n)
            if step == "gram":
                pe.wait_ge(S["kqn_ready"], n * 2 + 2)
                pe.wait_ge(S["wt_ready"], n)
                for hh in range(NH):
                    t = nc.tensor.transpose(r4(bank(7))[:, hh, :], kqn[:, hh, 0, :], ident[:, :])
                t.then_inc(S["kt_full"], 1)
                pe.wait_ge(S["vnew_ready"], n)
                for hh in range(NH):
                    t = nc.tensor.transpose(r4(bank(3))[:, hh, :], vv[:, par, hh, :], ident[:, :])
                t.then_inc(S["vt_full"], 1)
                pe.wait_ge(S["s_ready"], n * 4)
                for hh in range(NH):
                    t = nc.tensor.matmul(PS[:, 5 + hh // 2, (hh % 2) * 256:(hh % 2 + 1) * 256],
                                         kqn[:, hh, 0, :],
                                         kqn[:, hh, :, :].rearrange("p s t -> p (s t)"),
                                         start=True, stop=True)
                t.then_inc(S["gram_full"], 1)
            if step == "a1t":
                pe.wait_ge(S["am0_ready"], n + 1)
                pe.wait_ge(S["scln_ready"], R * 2 if par == 1 or first else R * 2 - 1)
                for hh in range(NH):
                    t = nc.tensor.transpose(r4(bank(2))[:, hh, :], am[:, 0, hh, :], ident[:, :])
                t.then_inc(S["a1t_full"], 1)
            if step[0] == "y":
                pe.wait_ge(S["x_ready"], n * LEVELS + l)
                if l > 1:
                    if l == 2:
                        pe.wait_ge(S["attn_ready"], n + 1)
                    else:
                        pe.wait_ge(S["t_ready"], n * 5 + l - 2)
                    for hh in range(NH):
                        t = nc.tensor.transpose(r4(bank(5))[:, hh, :], Xm[:, hh, :], ident[:, :])
                    t.then_inc(S["xt_full"], 1)
                pe.wait_ge(S["am_ready"], n * 6 + l)
                if l == 1:
                    pe.wait_ge(S["vb_ready"], n + 1)
                else:
                    pe.wait_ge(S["ym_ready"], n * 6 + l - 1)
                for hh in range(NH):
                    x = Xm[:, hh, :].rearrange("p (m e c) -> p m e c", e=2, c=1 << l)[:, :, 1, :]
                    t = nc.tensor.matmul(
                        bank(3)[:, hh * 64:(hh + 1) * 64].rearrange("p (m c) -> p m c", c=1 << l),
                        am[:, l % 2, hh, :], x, start=True, stop=True)
                t.then_inc(S["y_full"], 1)
            if step[0] == "x":
                pe.wait_ge(S["ym_ready"], n * 6 + l)
                if l == 1:
                    pe.wait_ge(S["t1_ready"], n + 1)
                    pe.wait_ge(S["on_ready"], n)
                else:
                    pe.wait_ge(S["t_ready"], n * 5 + l - 1)
                for hh in range(NH):
                    t = nc.tensor.matmul(bank(4)[:, hh * 64:(hh + 1) * 64], Tm[:, hh, :],
                                         Ym[:, hh, :], start=True, stop=True)
                t.then_inc(S["xy_full"], 1)
            if step == "w":
                pe.wait_ge(S["x_ready"], (n + 1) * LEVELS)
                pe.wait_ge(S["kbg_ready"], n + 1)
                if last:
                    pe.wait_ge(S["oo_ready"], n)
                else:
                    pe.wait_ge(S["rln_ready"], n + 2)
                for hh in range(NH):
                    t = nc.tensor.matmul(r4(bank(7))[:, hh, :], kbg[:, hh, :], Xm[:, hh, :],
                                         start=True, stop=True)
                t.then_inc(S["w_full"], 1)
            if step == "v":
                pe.wait_ge(S["ym_ready"], (n + 1) * 6)
                pe.wait_ge(S["wt_ready"], n + 1)
                pe.wait_ge(S["s_ready"], n * 4)
                for hh in range(NH):
                    nc.tensor.matmul(r4(bank(3))[:, hh, :], Xm[:, hh, :], vb[:, hh, :],
                                     start=True, stop=False)
                    t = nc.tensor.matmul(r4(bank(3))[:, hh, :], wt[:, hh, :], state[:, hh, :],
                                         start=False, stop=True)
                t.then_inc(S["vn_full"], 1)
            if step == "o":
                pe.wait_ge(S["vnew_ready"], n + 1)
                pe.wait_ge(S["qdec_ready"], n + 1)
                for hh in range(NH):
                    nc.tensor.matmul(r4(bank(4))[:, hh, :], ge[:, par, hh, :], state[:, hh, :],
                                     start=True, stop=False)
                    t = nc.tensor.matmul(r4(bank(4))[:, hh, :], dec[par][:, 1, hh, :],
                                         vnew[:, hh, :], start=False, stop=True)
                t.then_inc(S["o_full"], 1)
                pe.wait_ge(S["kdec_ready"], n + 1)
                for hh in range(NH):
                    t = nc.tensor.matmul(r4(bank(5))[:, hh, :], kdec[:, hh, :], vnew[:, hh, :],
                                         start=True, stop=True)
                t.then_inc(S["kv_full"], 1)
            if step == "y3" and not first:
                pe.wait_ge(S["kdec_ready"], n + 1)
                transpose_o(pe, n - 1)
            if step == "y4" and not last:
                if first:
                    pe.wait_ge(S["kdec_ready"], n + 1)
                else:
                    pe.wait_ge(S["oo_ready"], n)
                sums_gc(pe, n + 1, 1 - par)
            if step == "x5" and not last:
                sums_norm(pe, n + 1)
            if step == "y3" and par == 0 and not first:
                sc_sums(pe, R - 1, 1)
            if step == "o" and par == 1:
                sc_sums(pe, R, 0)

        def att_q(pe, R, c, dt, col_slice):
            if c == 1:
                pe.wait_ge(S["pt_out"], R * 2)
            for k in range(KT):
                product = col_slice(PS[:, (4 if c else 2) + dt, :], dt, c, k)
            product.then_inc(S["q_full"], 1)

        def att_pe(pe, half, j, col_slice, row_pass, norm):
            R = half * XH + j
            n_u = unit(half, U_ATT + j * 4)

            def scores(c):
                pe.wait_ge(S["q_out"], R * 4 + 2 * c + 2)
                pe.wait_ge(S["p_exp"], (R * 2 + c) * 4)
                for t in range(4):
                    ts = slice(c * CH + t * P, c * CH + (t + 1) * P)
                    for dt in range(2):
                        last = nc.tensor.matmul(
                            PS[:, 6 + t // 2, (t % 2) * N_MEM:(t % 2 + 1) * N_MEM], qT[:, dt, ts],
                            kmem[:, bass.ds(j * 2 + dt, 1), :].rearrange("p n m -> p (n m)"),
                            start=dt == 0, stop=dt == 1)
                last.then_inc(S["s_full"], 1)

            def transposes(c):
                pe.wait_ge(S["p_ready"], R * 2 + c + 1)
                if c == 0:
                    pe.wait_ge(S["q_out"], R * 4 + 4)
                else:
                    pe.wait_ge(S["pt_out"], R * 2 + 1)
                for t in range(4):
                    for m in range(2):
                        last = nc.tensor.transpose(PS[:, 4 + m, t * P:(t + 1) * P],
                                                   pp[:, t, m * P:(m + 1) * P], ident[:, :])
                last.then_inc(S["pt_full"], 1)

            def pv(c):
                pe.wait_ge(S["pt_out"], R * 2 + c + 1)
                if c == 0:
                    pe.wait_ge(S["vh_ready"], (R + 1) * 16)
                    for par in range(2):
                        pe.wait_ge(S[f"row_out{par}"], (half * ROW_PASSES + R_ATT + j) * 4)
                else:
                    pe.wait_ge(S["p_exp"], (R * 2 + 2) * 4)
                for dt in range(2):
                    for m in range(2):
                        last = nc.tensor.matmul(PS[:, 6 * c + dt, :],
                                                vh[:, m, dt * P:(dt + 1) * P], pT[:, m, :],
                                                start=m == 0, stop=m == 1)
                last.then_inc(S["pv_full"], 1)

            for par in range(2):
                pe.wait_ge(S[f"tr_lo{par}"], transposed(half, 2))
            att_q(pe, R, 1, 0, col_slice)
            scores(0)
            att_q(pe, R, 1, 1, col_slice)
            transposes(0)
            scores(1)
            pv(0)
            if norm is None:
                pe.wait_ge(S["w_lo_ready"], n_u + 6)
                att_q(pe, R + 1, 0, 0, col_slice)
            transposes(1)
            if norm is None:
                att_q(pe, R + 1, 0, 1, col_slice)
            pv(1)

            def ready(t):
                if t % 4 == 0:
                    pe.wait_ge(S["ot_lo"], R * 2 + t // 4 + 1)
                if t == 0:
                    pe.wait_ge(S["q_out"], R * 4 + (4 if norm is not None else 6))

            if norm is not None:
                pe.wait_ge(S["pt_out"], R * 2 + 2)
                pe.wait_ge(S["ot_lo"], R * 2 + 2)
            row_pass(half, half * ROW_PASSES + R_ATT + j, n_u + 2, [2, 3],
                     [row_hi[:, k, :] for k in (0, 1)], [row_lo[:, k, :] for k in (0, 1)],
                     ready, norm)


        block = ctx.enter_context(nc.Block())

        @block.sync
        def _(sp):
            def load_unit(n, source, slot):
                if not isinstance(n, int) or n >= 2:
                    sp.wait_ge(S["w_lo_ready"], n - 1)
                sp.dma_start(raw[slot][:, :], w_units[bass.ds(source, 1), :, :]
                             .rearrange("n p c -> p (n c)")).then_inc(S[f"raw_ready{slot}"], 16)

            def load_v(half, j):
                sp.wait_ge(S["pv_full"], (half * XH + j) * 2)
                sp.dma_start(vh[:, :, :], vmem_d[:, :, bass.ds(j * XD, XD)])\
                    .then_inc(S["vh_ready"], 16)

            def load_gain(g, before):
                sp.wait_ge(S["xn_ready"], before)
                sp.dma_start(gain[:, :], g[0:1, :].broadcast_to([P, D])).then_inc(S["gain_in"], 16)

            for dst, src in ((mem_in[:, :, :], mem.rearrange("(t p) c -> p t c", p=P)), (cw[:, :, :, :], conv_w), (scw[:, :, :], sc_w), (scg[:, :, :], sc_g),
                             (gdng[:, :], gdn_g),
                             (nega[:, :], a_log[0:1, :].broadcast_to([P, NH])),
                             (dtb[:, :], dt_bias[0:1, :].broadcast_to([P, NH]))):
                sp.dma_start(dst, src).then_inc(S["const_in"], 16)
            sp.dma_start(gain[:, :], g_mem[0:1, :].broadcast_to([P, D])).then_inc(S["gain_in"], 16)
            sp.wait_ge(S["const_made"], 9)
            sp.dma_start(raw[2][:, 0:KT * 8], w_ab).then_inc(S["wab_raw"], 16)
            for n in range(MEM_UNITS):
                load_unit(n, n, n % 2)
            sp.wait_ge(S["vm_out"], 1)
            sp.dma_start(vmem_d, vmem[:, :, :]).then_inc(S["vm_stored"], 16)

            with sp.Fori(0, NHALF) as half:
                for k in range(TT // 2):
                    sp.wait_ge(S["xn_ready"], half * (norm_no(0, 3, 2 * k + 1) + 1))
                    sp.dma_start(h[:, 2 * k:2 * k + 2, :], x[bass.ds(half * TT + 2 * k, 2), :, :]
                                 .rearrange("n p c -> p n c")).then_inc(S[f"h_in{k}"], 16)
                    if k == 1:
                        sp.wait_ge(S["row_full1"], half * ROW_PASSES * 4)
                        sp.dma_start(gain_mix[:, :], g_mix[0:1, :].broadcast_to([P, D]))\
                            .then_inc(S["gain_in"], 16)
                with sp.Fori(0, NH) as j:
                    for u in range(4):
                        load_unit(unit(half, U_QKVZ + j * 4 + u), MEM_UNITS + U_QKVZ + j * 4 + u,
                                  u % 2)
                load_gain(g_x, norm_no(half, 1, 0))
                with sp.Fori(0, 4) as j:
                    for u in range(3):
                        load_unit(unit(half, U_MIX + j * 3 + u), MEM_UNITS + U_MIX + j * 3 + u, u)
                for kk in range(KT):
                    load_unit(unit(half, U_OUT + kk), MEM_UNITS + U_OUT + kk, kk % 2)
                    if kk == 1:
                        sp.wait_ge(S["oo_ready"], (half + 1) * TT)
                        sp.wait_ge(S["y_stored"], (half + 1) * 16 * 8)
                        sp.wait_ge(S["o_stored"], (half + 1) * 16 * TT)
                        for k in range(2):
                            sp.wait_ge(S[f"mix_in{k}"], (half * KT // 2 + 1) * 16)
                        for k in range(TT // 2):
                            sp.dma_start(h[:, 2 * k:2 * k + 2, :],
                                         x[bass.ds(half * TT + 2 * k, 2), :, :]
                                         .rearrange("n p c -> p n c")).then_inc(S[f"h_in{k}"], 16)
                with sp.Fori(0, XH - 1) as j:
                    for u in range(4):
                        load_unit(unit(half, U_ATT + j * 4 + u), MEM_UNITS + U_ATT + j * 4 + u, u % 2)
                        if u == 2:
                            load_v(half, j)
                load_gain(g_ffn, norm_no(half, 2, 0))
                for u in range(4):
                    load_unit(unit(half, U_ATT + (XH - 1) * 4 + u), MEM_UNITS + U_ATT + (XH - 1) * 4 + u, u % 2)
                    if u == 2:
                        load_v(half, XH - 1)
                with sp.Fori(0, NPAIR - 1) as j:
                    for u in range(6):
                        load_unit(unit(half, U_FFN + j * 6 + u), MEM_UNITS + U_FFN + j * 6 + u, u % 2)
                for u in range(6):
                    load_unit(unit(half, U_FFN + (NPAIR - 1) * 6 + u), MEM_UNITS + U_FFN + (NPAIR - 1) * 6 + u, u % 2)
                load_gain(g_fin, norm_no(half, 3, 0))
            sp.wait_ge(S["out_stored"], NHALF * TT * 16)

        @block.gpsimd
        def _(pool):
            def made():
                return S["const_made"]

            def triangle(dst, base, pattern, mult, op=ALU.is_ge):
                pool.affine_select(out=dst, in_=dst, pattern=pattern, compare_op=op, fill=0.0,
                                   base=base, channel_multiplier=mult).then_inc(made(), 1)

            pool.memset(ones[:, :], 1.0).then_inc(made(), 1)
            pool.memset(three_halves[:, :], 1.5).then_inc(made(), 1)
            pool.memset(ident[:, :], 0.0).then_inc(made(), 1)
            pool.memset(group_ones[:, :], 0.0).then_inc(made(), 1)
            pool.memset(upto[:, :], 1.0).then_inc(made(), 1)
            pool.memset(level_mask[:, :, :], 0.0).then_inc(made(), 1)
            pool.memset(raw[2][:, :], 0.0).then_inc(made(), 1)
            pool.memset(halo[:, :, :, :], 0.0).then_inc(made(), 1)
            pool.memset(sc_halo[:, :, :], 0.0).then_inc(made(), 1)
            pool.memset(state[:, :, :], 0.0).then_inc(made(), 1)
            n = 10
            pool.wait_ge(made(), n)
            pool.affine_select(out=ident[:, :], in_=ident[:, :], pattern=[[-1, P]],
                               compare_op=ALU.not_equal, fill=1.0, base=0,
                               channel_multiplier=1).then_inc(made(), 1)
            triangle(upto[:, :], 0, [[1, P]], -1)
            n += 2
            for lo in (0, 64):
                pool.wait_ge(made(), n)
                pool.memset(group_ones[lo:lo + 64, lo:lo + 64], 1.0).then_inc(made(), 1)
                n += 1
            for l in range(LEVELS):
                b = 1 << l
                m = P // (2 * b)
                v = level_mask[:, l, :].rearrange("p (m e c) -> p m e c", e=2, c=b)[:, :, 0, :]
                pool.wait_ge(made(), n)
                pool.memset(v, 1.0).then_inc(made(), 1)
                n += 1
                pool.wait_ge(made(), n)
                triangle(v, -b, [[-2 * b, m], [0, b]], 1)
                n += 1
                pool.wait_ge(made(), n)
                triangle(v, 2 * b - 1, [[2 * b, m], [0, b]], -1)
                n += 1
            assert n == CONSTS

            def split_lo(n):
                number, slot, raw_slot = n
                pool.wait_ge(S["w_hi_ready"], number + 1)
                pool.tensor_tensor(w_lo[slot][:, :], raw[raw_slot][:, :],
                                   w_hi[slot][:, :].bitcast(f32), ALU.subtract)\
                    .then_inc(S["w_lo_ready"], 1)

            pool.wait_ge(S["wab_hi_ready"], 1)
            pool.tensor_tensor(wab_lo[:, :], raw[2][:, 0:KT * 8 + P], wab_hi[:, :].bitcast(f32),
                               ALU.subtract).then_inc(S["wab_lo_ready"], 1)
            for t in range(2):
                newton(pool, t, t)
            for n in range(MEM_UNITS):
                split_lo((n, n % RING, n % 2))

            with pool.Fori(0, NHALF) as half:
                newtons(pool, half, 0)
                for u in range(2):
                    split_lo((unit(half, U_QKVZ + u), u, u))
                with pool.Fori(0, NH) as j:
                    for u in range(4):
                        split_lo((unit(half, U_QKVZ + j * 4 + u + 2), (u + 2) % 4, u % 2))

                decays_pool(pool, half * TT, 0, 0)
                chunk_pool(pool, half, 0, 0, 0, False, split_lo)
                with pool.Fori(0, 3) as j:
                    chunk_pool(pool, half, j * 2 + 1, 1, j, False, split_lo)
                    chunk_pool(pool, half, j * 2 + 2, 0, j + 1, False, split_lo)
                chunk_pool(pool, half, TT - 1, 1, 3, True, split_lo)
                for i in range(KT // 2):
                    for k in range(2):
                        hi = w_hi[4 + k][:, :] if i % 2 == 0 else row_hi[:, k, :]
                        lo = w_lo[4 + k][:, :] if i % 2 == 0 else row_lo[:, k, :]
                        pool.wait_ge(S["mix_hi_ready"], half * KT + 2 * i + k + 1)
                        if i == 0:
                            pool.wait_ge(S["o_full"], (half + 1) * TT)
                        pool.tensor_tensor(lo, (mix_first if i == 0 else mixraw)[:, k, :], hi.bitcast(f32), ALU.subtract)\
                            .then_inc(S["mix_lo_ready"], 1)
                    for k in range(2):
                        split_lo((unit(half, U_OUT + 2 * i + k + 2), (2 * i + k + 2) % 4, k))
                newtons(pool, half, 1)
                with pool.Fori(0, XH) as j:
                    for u in range(4):
                        split_lo((unit(half, U_ATT + j * 4 + u + 2), (u + 2) % 4, u % 2))
                newtons(pool, half, 2)
                with pool.Fori(0, NPAIR - 1) as j:
                    ffn_pool(pool, half, j, split_lo, False)
                ffn_pool(pool, half, NPAIR - 1, split_lo, True)
                newtons(pool, half, 3)

        @block.scalar
        def _(act):
            def split_hi(load, slot, raw_slot):
                act.wait_ge(S[f"raw_ready{raw_slot}"], 16 * load)
                act.activation(w_hi[slot][:, :], raw[raw_slot][:, :], ACT.Copy)\
                    .then_inc(S["w_hi_ready"], 1)

            def norm_stats(src, squares, par, no):
                if not isinstance(no, int) or no >= 2:
                    act.wait_ge(S["xn_ready"], no - 1)
                act.activation(squares[:, :], src, ACT.Square, accum_out=stat["ss"][:, par:par + 1])\
                    .then_inc(S["ss_ready"], 1)
                act.wait_ge(S["ss_ready"], no + 1)
                act.activation(stat["t"][:, par:par + 1], stat["ss"][:, par:par + 1], ACT.Identity,
                               bias=EPS / 2, scale=0.5 / D)
                act.activation(stat["l"][:, par:par + 1], stat["ss"][:, par:par + 1], ACT.Ln,
                               bias=EPS, scale=1.0 / D).then_inc(S["ln_ready"], 1)
                act.wait_ge(S["ln_ready"], no + 1)
                act.activation(stat["y"][:, par:par + 1], stat["l"][:, par:par + 1], ACT.Exp,
                               scale=-0.5).then_inc(S["y_ready"], 1)

            def norm_hi(t, count):
                act.wait_ge(S[f"tr_full{t % 2}"], count + 1)
                act.activation(act_hi[:, :, t * P:(t + 1) * P],
                               bank(4 + 2 * (t % 2), 2).rearrange("p b (k t) -> p (b k) t", k=4),
                               ACT.Copy).then_inc(S["tr_hi"], 1)

            def norm_act(half, which, ready):
                def hi(t):
                    if t == 0:
                        act.wait_ge(S["out_stored"], 16 * half * TT)
                    norm_hi(t, transposed(half, which) + t // 2)

                for s in range(TT + 2):
                    if s >= 2 and which in (1, 2):
                        hi(s - 2)
                    if s < TT:
                        ready(s)
                        norm_stats(h[:, s, :], junk_last if which == 3 else junk, s % 2,
                                   norm_no(half, which, s))
                    if s >= 2 and which == 0:
                        hi(s - 2)
                    if s >= 2 and which == 3:
                        t = s - 2
                        act.wait_ge(S["xn_ready"], norm_no(half, 3, t) + 1)
                        act.dma_start(out[bass.ds(half * TT + t, 1), :, :]
                                      .rearrange("n p c -> p (n c)"), result[:, t, :])\
                            .then_inc(S["out_stored"], 16)

            act.preload_act_table_set("natural_log_exp_and_others")
            act.wait_ge(S["const_in"], 7 * 16)
            act.activation(nega[:, :], nega[:, :], ACT.Exp).then_inc(S["nega_ready"], 1)
            act.wait_ge(S["nega_ready"], 1)
            act.activation(nega[:, :], nega[:, :], ACT.Copy, scale=-1.0)\
                .then_inc(S["nega_ready"], 1)
            act.wait_ge(S["wab_raw"], 16)
            act.activation(wab_hi[:, :], raw[2][:, 0:KT * 8 + P], ACT.Copy)\
                .then_inc(S["wab_hi_ready"], 1)
            for t in range(2):
                norm_stats(mem_in[:, t, :], junk, t, t)
            for t in range(2):
                norm_hi(t, 0)
            for n in range(MEM_UNITS):
                if RING <= n < RING + KT:
                    act.wait_ge(S[f"km_full{n % 2}"], (n - RING) // 2 + 1)
                elif n >= RING + KT:
                    act.wait_ge(S["vm_full"], n - RING - KT + 1)
                split_hi(n // 2 + 1, n % RING, n % 2)
            act.wait_ge(S["vm_full"], KT)
            act.activation(flat(vmem[:, :, :]), flat(bank(4, 4)), ACT.Copy)\
                .then_inc(S["vm_out"], 1)

            with act.Fori(0, NHALF) as half:
                act.preload_act_table_set("natural_log_exp_and_others")
                norm_act(half, 0, lambda t: act.wait_ge(S[f"h_in{t // 2}"], 32 * half + 16))
                for u in range(2):
                    split_hi(nth_load(half, L_QKVZ), u, u)
                act.wait_ge(S["vm_stored"], 16)
                for c in range(NCH):
                    act.wait_ge(S[f"ab_full{c}"], half + 1)
                    act.activation(ab_t[:, c * CH:(c + 1) * CH], PS[:, c, :], ACT.Copy)\
                        .then_inc(S["ab_out"], 1)
                gates_act(act, half)

                act.preload_act_table_set("silu_and_others")
                with act.Fori(0, NH) as j:
                    R = half * NH + j
                    for u in range(4):
                        split_hi(nth_load(half, L_QKVZ + j * 2 + u // 2 + 1), (u + 2) % 4, u % 2)
                        for c in range(NCH):
                            g = u * 2 + c
                            b = g % 4
                            if u < 3:
                                if c == 0:
                                    act.wait_ge(S["halo_out"], 3 * R + u - 1 if u >= 2
                                                else 3 * R)
                                act.wait_ge(S[f"qkvz_full{b}"], R * 2 + g // 4 + 1)
                                act.activation(conv_in[u % 2][:, 3 + c * CH:3 + (c + 1) * CH],
                                               bank(b), ACT.Copy).then_inc(S[f"qkvz_out{b}"], 1)
                                if g > 0:
                                    silu_store(act, half, j, R, g - 1)
                            else:
                                if c == 0:
                                    silu_store(act, half, j, R, g - 1)
                                silu_z(act, half, j, R, g)
                act.preload_act_table_set("natural_log_exp_and_others")
                gates_act_late(act, half)

                act.wait_ge(S["halo_out"], (half + 1) * NH * 3)
                act.wait_ge(S["st_stored0"], (half + 1) * NH * 4 * 16)
                act.wait_ge(S["st_stored1"], (half + 1) * NH * 4 * 16)
                start_act(act, half)
                chunk_act(act, half, 0, 0, 0, True, False, split_hi)
                with act.Fori(0, 3) as j:
                    chunk_act(act, half, j * 2 + 1, 1, j, False, False, split_hi)
                    chunk_act(act, half, j * 2 + 2, 0, j + 1, False, False, split_hi)
                chunk_act(act, half, TT - 1, 1, 3, False, True, split_hi)
                end_act(act, half)

                for i in range(KT // 2):
                    for k in range(2):
                        kk = 2 * i + k
                        slot = w_hi[4 + k][:, :] if i % 2 == 0 else row_hi[:, k, :]
                        act.wait_ge(S[f"mix_in{k}"], (half * KT // 2 + i + 1) * 16)
                        act.activation(slot, (mix_first if i == 0 else mixraw)[:, k, :], ACT.Copy)\
                            .then_inc(S["mix_hi_ready"], 1)
                    act.wait_ge(S["row_full1"], (half * ROW_PASSES + i) * 4)
                    for k in range(2):
                        split_hi(nth_load(half, L_OUT + i + 1), (2 * i + k + 2) % 4, k)
                    if i == 0:
                        act.wait_ge(S["oo_ready"], (half + 1) * TT)
                        act.wait_ge(S["y_stored"], (half + 1) * 16 * 8)
                        act.wait_ge(S["o_stored"], (half + 1) * 16 * TT)
                    if i < KT // 2 - 1:
                        for k in range(2):
                            act.wait_ge(S["mix_lo_ready"], half * KT + 2 * i + k + 1)
                            load_mix(act, half, 2 * i + 2 + k)
                act.wait_ge(S["mix_lo_ready"], (half + 1) * KT)
                act.wait_ge(S["row_full1"], (half * ROW_PASSES + KT // 2 - 1) * 4)
                norm_act(half, 1, lambda t: act.wait_ge(
                    S[f"row_out{t % 2}"], (half * ROW_PASSES + KT // 2 - 1) * 4 + t // 2 + 1))

                for g in range(2):
                    att_q_out(act, half * XH, g, half * XH * 2)
                with act.Fori(0, XH - 1) as j:
                    att_act(act, half, j, split_hi, False)
                att_act(act, half, XH - 1, split_hi, True)
                act.wait_ge(S["s_full"], (half + 1) * XH * 2)
                norm_act(half, 2, lambda t: act.wait_ge(
                    S[f"row_out{t % 2}"], (half * ROW_PASSES + R_ATT + XH - 1) * 4 + t // 2 + 1))

                act.preload_act_table_set("silu_and_others")
                with act.Fori(0, NPAIR - 1) as j:
                    ffn_act(act, half, j, split_hi, False)
                ffn_act(act, half, NPAIR - 1, split_hi, True)
                act.preload_act_table_set("natural_log_exp_and_others")
                for c in range(2):
                    act.wait_ge(S[f"al_ready{c}"], (half + 1) * NPAIR * 2)
                norm_act(half, 3, lambda t: act.wait_ge(
                    S[f"row_out{t % 2}"], (half * ROW_PASSES + ROW_PASSES - 1) * 4 + t // 2 + 1))

        @block.vector
        def _(dve):
            def norm_tile(src, dst, gain, par, no):
                dve.wait_ge(S["nstat"], no * 4 + 4)
                dve.scalar_tensor_tensor(dst, src, stat["r"][:, par:par + 1], gain[:, :],
                                         ALU.mult, ALU.mult).then_inc(S["xn_ready"], 1)

            def norm_lo(t, hi_count):
                dve.wait_ge(S["tr_hi"], hi_count + 1)
                dve.tensor_tensor(act_lo[:, :, t * P:(t + 1) * P],
                                  bank(4 + 2 * (t % 2), 2).rearrange("p b (k t) -> p (b k) t", k=4),
                                  act_hi[:, :, t * P:(t + 1) * P].bitcast(f32), ALU.subtract)\
                    .then_inc(S[f"tr_lo{t % 2}"], 1)

            def row_add(t, rp):
                dve.wait_ge(S[f"row_full{t % 2}"], rp * 4 + t // 2 + 1)
                dve.wait_ge(S[f"row_out{t % 2}"], rp * 4)
                dve.tensor_tensor(h[:, t, :], h[:, t, :], flat(bank(2 * (t % 2), 2)), ALU.add)\
                    .then_inc(S[f"row_out{t % 2}"], 1)

            def norm_dve(half, which, rp):
                for s in range(TT + 3):
                    if s < TT and rp is not None:
                        row_add(s, rp)
                    if s >= 3 and which < 3:
                        norm_lo(s - 3, 2 + (half * 3 + which) * TT + s - 3)
                    if 1 <= s <= TT:
                        t = s - 1
                        if which < 3:
                            dve.wait_ge(S[f"tr_full{t % 2}"], transposed(half, which) + t // 2)
                        norm_tile(h[:, t, :], result[:, t, :] if which == 3 else xn[:, t % 2, :],
                                  gain_mix if which == 0 else gain, t % 2,
                                  norm_no(half, which, t))

            dve.wait_ge(S["gain_in"], 16)
            for t in range(2):
                norm_tile(mem_in[:, t, :], xn[:, t, :], gain, t, t)
            for t in range(2):
                norm_lo(t, t)
            for u in range(KT):
                b = u % 2
                dve.wait_ge(S[f"km_full{b}"], u // 2 + 1)
                dve.tensor_copy(kmem[:, u, :], PS[:, b, 0:N_MEM]).then_inc(S[f"km_out{b}"], 1)
            dve.wait_ge(S["const_made"], CONSTS)

            with dve.Fori(0, NHALF) as half:
                dve.wait_ge(S["gain_in"], (half * 4 + 2) * 16)
                norm_dve(half, 0, None)
                gates_dve(dve, half, False)
                with dve.Fori(0, NH) as j:
                    R = half * NH + j
                    for u in range(3):
                        ci = conv_in[u % 2]
                        dve.wait_ge(S["halo_out"], 3 * R + u - 1 if u >= 2 else 3 * R)
                        dve.tensor_copy(ci[:, 0:3], halo[:, bass.ds(j, 1), u, :]
                                        .rearrange("p n k -> p (n k)")).then_inc(S["halo_in"], 1)
                        for c in range(NCH):
                            g = u * 2 + c
                            conv_dve(dve, R, j, u, c, g, ci)
                        dve.tensor_copy(halo[:, bass.ds(j, 1), u, :]
                                        .rearrange("p n k -> p (n k)"), ci[:, HALF:HALF + 3])\
                            .then_inc(S["halo_out"], 1)
                gates_dve(dve, half, True)
                start_dve(dve, half)
                chunk_dve(dve, half, 0, 0, 0, True, False)
                with dve.Fori(0, 3) as j:
                    chunk_dve(dve, half, j * 2 + 1, 1, j, False, False)
                    chunk_dve(dve, half, j * 2 + 2, 0, j + 1, False, False)
                chunk_dve(dve, half, TT - 1, 1, 3, False, True)
                end_dve(dve, half)
                for i in range(KT // 2 - 1):
                    for t in range(TT):
                        if i == 0 and t % 2 == 0:
                            dve.wait_ge(S[f"h_in{t // 2}"], (half + 1) * 32)
                        row_add(t, half * ROW_PASSES + i)
                dve.wait_ge(S["gain_in"], (half * 4 + 3) * 16)
                norm_dve(half, 1, half * ROW_PASSES + KT // 2 - 1)
                with dve.Fori(0, XH - 1) as j:
                    att_dve(dve, half, j)
                    for t in range(TT):
                        row_add(t, half * ROW_PASSES + R_ATT + j)
                att_dve(dve, half, XH - 1)
                dve.wait_ge(S["gain_in"], (half * 4 + 4) * 16)
                norm_dve(half, 2, half * ROW_PASSES + R_ATT + XH - 1)
                with dve.Fori(0, NPAIR - 1) as j:
                    ffn_dve(dve, half, j)
                    for t in range(TT):
                        row_add(t, half * ROW_PASSES + R_FFN + j)
                ffn_dve(dve, half, NPAIR - 1)
                dve.wait_ge(S["gain_in"], (half * 4 + 5) * 16)
                norm_dve(half, 3, half * ROW_PASSES + ROW_PASSES - 1)

        @block.tensor
        def _(pe):
            def three(out_ap, whi, wlo, xhi, xlo, start, stop):
                nc.tensor.matmul(out_ap, whi, xhi, start=start, stop=False)
                nc.tensor.matmul(out_ap, whi, xlo, start=False, stop=False)
                return nc.tensor.matmul(out_ap, wlo, xhi, start=False, stop=stop)

            def col_slice(out_ap, slot, c, k, width=CH):
                ks = slice(k * P, (k + 1) * P)
                cs = slice(c * CH, c * CH + width)
                return three(out_ap, w_hi[slot][:, ks], w_lo[slot][:, ks],
                             act_hi[:, k, cs], act_lo[:, k, cs], k == 0, k == KT - 1)

            def transpose_tile(t, count, xn_count):
                pe.wait_ge(S["xn_ready"], xn_count + 1)
                pe.wait_ge(S[f"tr_lo{t % 2}"], count)
                for k in range(KT):
                    last = nc.tensor.transpose(PS[:, 4 + 2 * (t % 2) + k // 4,
                                                  (k % 4) * P:(k % 4 + 1) * P],
                                               xn[:, t % 2, k * P:(k + 1) * P], ident[:, :])
                last.then_inc(S[f"tr_full{t % 2}"], 1)

            def row_pass(half, rp, n_u, slots, a_hi, a_lo, ready, norm=None):
                pe.wait_ge(S["w_lo_ready"], n_u + 2)
                for s in range(TT + 2):
                    if s < TT:
                        t = s
                        ready(t)
                        pe.wait_ge(S[f"row_out{t % 2}"], rp * 4 + t // 2)
                        for nh in range(2):
                            ts = slice(t * P, (t + 1) * P)
                            ns = slice(nh * CH, (nh + 1) * CH)
                            out_ap = PS[:, 2 * (t % 2) + nh, :]
                            for i in range(2):
                                nc.tensor.matmul(out_ap, a_hi[i][:, ts], w_hi[slots[i]][:, ns],
                                                 start=i == 0, stop=False)
                                nc.tensor.matmul(out_ap, a_hi[i][:, ts], w_lo[slots[i]][:, ns],
                                                 start=False, stop=False)
                                last = nc.tensor.matmul(out_ap, a_lo[i][:, ts],
                                                        w_hi[slots[i]][:, ns],
                                                        start=False, stop=i == 1)
                        last.then_inc(S[f"row_full{t % 2}"], 1)
                    if norm is not None and 2 <= s < TT + 1:
                        transpose_tile(s - 2, transposed(half, norm) + (s - 2) // 2,
                                       norm_no(half, norm, s - 2))

            def transpose_last(half, norm):
                transpose_tile(TT - 1, transposed(half, norm) + TT // 2 - 1,
                               norm_no(half, norm, TT - 1))

            def ffn_pe(half, j, first):
                R = half * NPAIR + j
                n_u = unit(half, U_FFN + j * 6)
                for f in range(2):
                    pe.wait_ge(S["w_lo_ready"], n_u + 2 * f + 2)
                    for c in range(2):
                        pe.wait_ge(S[f"ga_ready{c}"], R * 2 + f)
                        if c == 1:
                            pe.wait_ge(S["tr_lo1"], transposed(half, 3))
                        for k in range(KT):
                            col_slice(PS[:, 4 + 2 * c, :], 2 * f, c, k)
                        if first and f == 0 and c == 0:
                            transpose_last(half, 2)
                        for k in range(KT):
                            last = col_slice(PS[:, 5 + 2 * c, :], 2 * f + 1, c, k)
                        last.then_inc(S[f"gu_full{c}"], 1)

                def ready(t):
                    if t % 4 == 0:
                        pe.wait_ge(S[f"al_ready{t // 4}"], R * 2 + 2)

                row_pass(half, half * ROW_PASSES + R_FFN + j, n_u + 4, [4, 5],
                         [row_hi[:, k, :] for k in (0, 1)], [row_lo[:, k, :] for k in (0, 1)],
                         ready)

            pe.wait_ge(S["const_made"], CONSTS)
            for t in range(2):
                transpose_tile(t, 0, t)
            for t in range(2):
                pe.wait_ge(S[f"tr_lo{t}"], 1)
            for u in range(KT):
                b = u % 2
                pe.wait_ge(S["w_lo_ready"], u + 1)
                pe.wait_ge(S[f"km_out{b}"], u // 2)
                for k in range(KT):
                    last = col_slice(PS[:, b, 0:N_MEM], u % RING, 0, k, N_MEM)
                last.then_inc(S[f"km_full{b}"], 1)
            for k in range(KT):
                n = KT + k
                pe.wait_ge(S["w_lo_ready"], n + 1)
                for m in range(2):
                    for nh in range(2):
                        ms = slice(m * P, (m + 1) * P)
                        ns = slice(nh * CH, (nh + 1) * CH)
                        last = three(PS[:, 4 + 2 * m + nh, :], act_hi[:, k, ms], act_lo[:, k, ms],
                                     w_hi[n % RING][:, ns], w_lo[n % RING][:, ns],
                                     k == 0, k == KT - 1)
                last.then_inc(S["vm_full"], 1)
            pe.wait_ge(S["vm_out"], 1)

            with pe.Fori(0, NHALF) as half:
                for c in range(2):
                    pe.wait_ge(S[f"ga_ready{c}"], half * NPAIR * 2)
                for par in range(2):
                    pe.wait_ge(S[f"row_out{par}"], half * ROW_PASSES * 4)
                for b in range(2):
                    pe.wait_ge(S[f"km_out{b}"], KT // 2)
                pe.wait_ge(S["wab_lo_ready"], 1)
                for c in range(NCH):
                    for t in range(6 * c, 6 + 2 * c):
                        transpose_tile(t, transposed(half, 0) + t // 2, norm_no(half, 0, t))
                    for par in range(2):
                        pe.wait_ge(S[f"tr_lo{par}"], transposed(half, 0) + 2 + 2 * c)
                    for k in range(KT):
                        ks = slice(k * 8, k * 8 + P)
                        cs = slice(c * CH, (c + 1) * CH)
                        last = three(PS[:, c, :], wab_hi[:, ks], wab_lo[:, ks],
                                     act_hi[:, k, cs], act_lo[:, k, cs], k == 0, k == KT - 1)
                    last.then_inc(S[f"ab_full{c}"], 1)
                pe.wait_ge(S["ab_out"], (half + 1) * 2)
                for t in range(TT):
                    last = nc.tensor.transpose(PS[:, 6 + t // 4, t % 4 * P:(t % 4 + 1) * P],
                                               ab_t[:, t * P:(t + 1) * P], ident[:, :])
                last.then_inc(S["abt_full"], 1)

                with pe.Fori(0, NH) as j:
                    R = half * NH + j
                    for u in range(4):
                        n = unit(half, U_QKVZ + j * 4 + u)
                        pe.wait_ge(S["w_lo_ready"], n + 1)
                        for c in range(NCH):
                            g = u * 2 + c
                            b = g % 4
                            if g >= 4:
                                pe.wait_ge(S[f"qkvz_out{b}"], CONV_OUT[g - 4] + R * CONV_OUT_PER[b])
                            else:
                                pe.wait_ge(S["stage_ready"], R * 8)
                                pe.wait_ge(S[f"qkvz_out{b}"], R * CONV_OUT_PER[b])
                            for k in range(KT):
                                last = col_slice(PS[:, b, :], u, c, k)
                            last.then_inc(S[f"qkvz_full{b}"], 1)
                pe.wait_ge(S["stage_ready"], (half + 1) * NH * 8)

                for b in range(4):
                    pe.wait_ge(S[f"qkvz_out{b}"], (half + 1) * NH * CONV_OUT_PER[b])
                pe.wait_ge(S["gate_step_dve"], half * GATE_DVE + GD["g"])
                nc.tensor.matmul(PS[:, 7, 0:TT * NH], upto[:, :], flat(G["g"][:, :, :]),
                                 start=True, stop=True)
                nc.tensor.matmul(PS[:, 7, TT * NH:2 * TT * NH], ones[:, :], flat(G["g"][:, :, :]),
                                 start=True, stop=True).then_inc(S["gate_gc_full"], 1)

                def chunk_pe(m, par, j, first, last):
                    R = half * 4 + j
                    n_u = unit(half, U_MIX + j * 3)
                    done = par * CHUNK_SLICES
                    for step, fill in zip(STEPS, FILL_FIRST if first else FILL):
                        chunk_step_pe(pe, half, m, par, j, step, first, last)
                        for s in range(done, done + fill):
                            u, c, k = s // (NCH * KT), s // KT % NCH, s % KT
                            if k == 0:
                                if c == 0:
                                    pe.wait_ge(S["w_lo_ready"], n_u + u + 1)
                                if u == 0:
                                    pe.wait_ge(S[f"scy_ready{c}"], R)
                                elif u == 1:
                                    pe.wait_ge(S["c_out"], R * 2 + c + 1)
                                else:
                                    pe.wait_ge(S["u_ready"], R * 2 + c + 1)
                            product = col_slice(PS[:, c, :], u, c, k)
                            if k == KT - 1:
                                product.then_inc(S[f"sc_full{c}"], 1)
                        done += fill

                pe.wait_ge(S["gate_step_dve"], half * GATE_DVE + GD["gl"])
                chunk_pe(0, 0, 0, True, False)
                with pe.Fori(0, 3) as j:
                    chunk_pe(j * 2 + 1, 1, j, False, False)
                    chunk_pe(j * 2 + 2, 0, j + 1, False, False)
                chunk_pe(TT - 1, 1, 3, False, True)
                n = half * TT + TT - 1
                sc_sums(pe, half * 4 + 3, 1)
                pe.wait_ge(S["wt_ready"], n + 1)
                transpose_o(pe, n)

                pe.wait_ge(S["scyn_ready"], (half + 1) * 8)
                pe.wait_ge(S["vnew_ready"], (half + 1) * TT)
                for i in range(KT // 2):
                    even = i % 2 == 0
                    hi = [w_hi[4][:, :], w_hi[5][:, :]] if even else [row_hi[:, k, :] for k in (0, 1)]
                    lo = [w_lo[4][:, :], w_lo[5][:, :]] if even else [row_lo[:, k, :] for k in (0, 1)]
                    final = i == KT // 2 - 1
                    n_u = unit(half, U_OUT + 2 * i)

                    def ready(t, i=i):
                        if t == 0:
                            pe.wait_ge(S["mix_lo_ready"], half * KT + 2 * i + 2)

                    if final:
                        pe.wait_ge(S["oo_ready"], (half + 1) * TT)
                        pe.wait_ge(S["s_ready"], (half + 1) * TT * 4)
                    row_pass(half, half * ROW_PASSES + i, n_u, [2 * i % 4, 2 * i % 4 + 1], hi, lo,
                             ready, 1 if final else None)

                for par in range(2):
                    pe.wait_ge(S[f"tr_lo{par}"], transposed(half, 1) + 2)
                pe.wait_ge(S["row_out1"], (half * ROW_PASSES + KT // 2) * 4)
                pe.wait_ge(S["w_lo_ready"], unit(half, U_ATT) + 2)
                att_q(pe, half * XH, 0, 0, col_slice)
                transpose_last(half, 1)
                att_q(pe, half * XH, 0, 1, col_slice)
                with pe.Fori(0, XH - 1) as j:
                    att_pe(pe, half, j, col_slice, row_pass, None)
                att_pe(pe, half, XH - 1, col_slice, row_pass, 2)

                pe.wait_ge(S["tr_lo0"], transposed(half, 3))
                pe.wait_ge(S["tr_lo1"], transposed(half, 2) + 2)
                ffn_pe(half, 0, True)
                with pe.Fori(0, NPAIR - 1) as j:
                    ffn_pe(half, j + 1, False)


_VECTORS = {"g_mix": "norm_mix_g", "g_mem": "norm_mem_g", "g_x": "norm_x_g",
            "g_ffn": "norm_ffn_g", "g_fin": "norm_final_g"}


def _units(inputs):
    import numpy as np

    def columns(w, first, count):
        w = w[:, first:first + count * P].reshape(KT, P, count, P)
        return w.transpose(2, 1, 0, 3).reshape(count, P, D)

    def rows(w):
        return w.reshape(-1, P, D)

    w = {k: np.asarray(inputs[k])[0] for k in
         ("w_in", "w_out", "w_xq", "w_xk", "w_xv", "w_xo", "w_gate", "w_up", "w_down")}
    width = NH * HD
    q, k, v, z = (columns(w["w_in"], i * width, NH) for i in range(4))
    first = 4 * width + 2 * NH
    b, c, hh = (columns(w["w_in"], first + i * width, 4) for i in range(3))
    wo = rows(w["w_out"])
    xq, xo = columns(w["w_xq"], 0, KT), rows(w["w_xo"])
    gate, up, down = columns(w["w_gate"], 0, FF // P), columns(w["w_up"], 0, FF // P), rows(w["w_down"])
    parts = [columns(w["w_xk"], 0, KT), rows(w["w_xv"])]
    parts += [np.stack([q, k, v, z], 1).reshape(-1, P, D)]
    parts += [np.stack([c, hh, b], 1).reshape(-1, P, D)]
    parts += [np.concatenate([wo[4:], wo[:4]])]
    parts += [np.concatenate([xq.reshape(XH, 2, P, D), xo.reshape(XH, 2, P, D)], 1)
              .reshape(-1, P, D)]
    parts += [np.concatenate([np.stack([gate, up], 1).reshape(NPAIR, 4, P, D),
                              down.reshape(NPAIR, 2, P, D)], 1).reshape(-1, P, D)]
    units = np.concatenate(parts)
    ab = w["w_in"][:, 4 * width:first].reshape(KT, P, 2 * NH).transpose(1, 0, 2).reshape(P, -1)
    return units, ab


def kernel(**inputs):
    import numpy as np
    import concourse.bacc as bacc
    from concourse.bass_utils import run_bass_kernel_spmd

    a = {k: np.asarray(v) for k, v in inputs.items()}
    units, ab = _units(a)
    arrays = {
        "x": a["x"].reshape(SEQ // P, P, D),
        "mem": a["mem"].reshape(N_MEM, D),
        "w_units": units,
        "w_ab": ab,
        "conv_w": a["conv_qkv_w"][0].reshape(4, 3, NH, P).transpose(3, 2, 1, 0),
        "sc_w": a["conv_sc_w"][0].reshape(3, 4, P).transpose(2, 1, 0),
        "a_log": a["a_log"].reshape(1, NH),
        "dt_bias": a["dt_bias"].reshape(1, NH),
        "gdn_g": a["gdn_norm_g"].reshape(P, 1),
        "sc_g": a["sc_norm_g"].reshape(4, P, 1).transpose(1, 0, 2),
    }
    for name, source in _VECTORS.items():
        arrays[name] = a[source].reshape(1, D)
    arrays = {k: np.ascontiguousarray(v) for k, v in arrays.items()}
    nc = bacc.Bacc("TRN2", target_bir_lowering=False, num_devices=1)
    aps = {k: nc.dram_tensor("in_" + k, v.shape, mybir.dt.from_np(v.dtype),
                             kind="ExternalInput").ap() for k, v in arrays.items()}
    out = nc.dram_tensor("out", (SEQ // P, P, D), f32, kind="ExternalOutput").ap()
    block_kernel(nc, out=out, **aps)
    r = run_bass_kernel_spmd(nc, [{"in_" + k: v for k, v in arrays.items()}], core_ids=[0])
    return r.results[0]["out"].reshape(1, SEQ, D)
```
